# Optimizing a Trainium2 kernel written in Bass

```python
import jax, jax.numpy as jnp
from jax import lax
import numpy as np

'''One inference step of a 4-layer hybrid streaming encoder (parallel head groups).

Each layer: x += 1/2 SwiGLU(RMSNorm(x)); h = RMSNorm(x); one combined input projection of h
is split between (A) a short gated depthwise width-3 causal convolution mixer (8 channel groups)
and (B) an mLSTM matrix-memory mixer (4 heads, chunkwise-parallel, exactly per-token causal);
each group's output is normalised per group / head, concatenated, and sent through one output
projection added to the residual; then x += 1/2 SwiGLU(RMSNorm(x)). A final RMSNorm closes the trunk.

Inputs:
  x_prompt   (BATCH, SEQ, D_MODEL)          first SEQ frames of BATCH new streams (no history)
  x_sample   (DEC_BATCH, DEC_SEQ, D_MODEL)  next DEC_SEQ frames of DEC_BATCH running streams
  cache_conv (DEPTH, DEC_BATCH, CONV_K-1, CONV_W)       last 2 conv input rows (C * x_in)
  state_C    (DEPTH, DEC_BATCH, M_HEADS, M_DK, M_DV)    stabilised mLSTM matrix memory
  state_n    (DEPTH, DEC_BATCH, M_HEADS, M_DK)          stabilised mLSTM normaliser
  state_m    (DEPTH, DEC_BATCH, M_HEADS)                mLSTM running-max stabiliser
  then the weights (stacked over DEPTH).
Output tuple:
  (y_prompt (BATCH,SEQ,D_MODEL), y_sample (DEC_BATCH,DEC_SEQ,D_MODEL),
   prompt_conv (DEPTH,BATCH,2,CONV_W), prompt_C (DEPTH,BATCH,H,DK,DV), prompt_n (DEPTH,BATCH,H,DK), prompt_m (DEPTH,BATCH,H),
   sample_conv (DEPTH,DEC_BATCH,2,CONV_W), sample_C, sample_n, sample_m (same with DEC_BATCH))
'''

D_MODEL = 1024
BATCH = 1
SEQ = 1024
DEPTH = 1
DEC_BATCH = 1
DEC_SEQ = 32
PAST_LEN = 512

CHUNK = 64
D_MIX = D_MODEL
CONV_W = D_MIX // 2
CONV_GROUPS = 8
CONV_GROUP_DIM = CONV_W // CONV_GROUPS
CONV_K = 3
M_HEADS = 4
M_DV = (D_MIX - CONV_W) // M_HEADS
M_DK = M_DV // 2
D_FF = ((8 * D_MODEL // 3 + 127) // 128) * 128
N_IN = 3 * CONV_W + 2 * M_HEADS * M_DK + 2 * M_HEADS * M_DV + 2 * M_HEADS
EPS = 1e-6

kernel_name = 'hybrid_conv_mlstm_macaron_stream_step'

def _rmsnorm(x, g):
    xf = x.astype(jnp.float32)
    y = xf * lax.rsqrt(jnp.mean(xf * xf, axis=-1, keepdims=True) + EPS)
    return (y * g.astype(jnp.float32)).astype(x.dtype)

def _swiglu(x, w_gate, w_up, w_down):
    return (jax.nn.silu(x @ w_gate) * (x @ w_up)) @ w_down

def _mlstm_chunk(carry, inp):
    C, n, m = carry
    q, k, v, li, lf = inp
    L = q.shape[2]
    b = jnp.cumsum(lf, axis=-1)
    causal = jnp.tril(jnp.ones((L, L), dtype=bool))
    d_log = b[..., :, None] - b[..., None, :] + li[..., None, :]
    d_log = jnp.where(causal, d_log, -jnp.inf)
    inter = b + m[..., None]
    m_t = jnp.maximum(inter, jnp.max(d_log, axis=-1))
    w_intra = jnp.exp(d_log - m_t[..., None])
    w_inter = jnp.exp(inter - m_t)
    s = jnp.einsum('bhtd,bhsd->bhts', q, k) * w_intra
    num = jnp.einsum('bhts,bhsv->bhtv', s, v) + w_inter[..., None] * jnp.einsum('bhtd,bhdv->bhtv', q, C)
    den = jnp.sum(s, axis=-1) + w_inter * jnp.einsum('bhtd,bhd->bht', q, n)
    h = num / jnp.maximum(jnp.abs(den), jnp.exp(-m_t))[..., None]
    b_last = b[..., -1]
    g = b_last[..., None] - b + li
    m_new = jnp.maximum(b_last + m, jnp.max(g, axis=-1))
    wk = jnp.exp(g - m_new[..., None])
    decay = jnp.exp(b_last + m - m_new)
    C_new = decay[..., None, None] * C + jnp.einsum('bhs,bhsd,bhsv->bhdv', wk, k, v)
    n_new = decay[..., None] * n + jnp.einsum('bhs,bhsd->bhd', wk, k)
    return (C_new, n_new, m_new), h

def _mlstm(q, k, v, li, lf, C0, n0, m0):
    bsz, T = q.shape[0], q.shape[1]
    L = min(CHUNK, T)
    nc = T // L
    f32 = jnp.float32

    def to_chunks(a):
        a = a.astype(f32).reshape((bsz, nc, L) + a.shape[2:])
        return jnp.moveaxis(jnp.swapaxes(a, 2, 3), 1, 0)

    xs = (to_chunks(q) * (M_DK ** -0.5), to_chunks(k), to_chunks(v), to_chunks(li), to_chunks(lf))
    carry0 = (C0.astype(f32), n0.astype(f32), m0.astype(f32))
    (C, n, m), h = lax.scan(_mlstm_chunk, carry0, xs)
    h = jnp.swapaxes(jnp.moveaxis(h, 0, 1), 2, 3).reshape(bsz, T, M_HEADS, M_DV)
    return h, C, n, m

def _mixer(h, conv_prev, C0, n0, m0, w_in, b_igate, b_fgate, conv_w, conv_b, g_conv, g_mlstm, w_out):
    bsz, T, _ = h.shape
    sizes = [CONV_W, CONV_W, CONV_W, M_HEADS * M_DK, M_HEADS * M_DK, M_HEADS * M_DV, M_HEADS * M_DV, M_HEADS, M_HEADS]
    offs = np.cumsum(sizes)[:-1].tolist()
    p = h @ w_in
    bg, cg, xin, q, k, v, o, ip, fp = jnp.split(p, offs, axis=-1)
    u = cg * xin
    u_pad = jnp.concatenate([conv_prev.astype(u.dtype), u], axis=1)
    y = conv_b + conv_w[0] * u_pad[:, :-2] + conv_w[1] * u_pad[:, 1:-1] + conv_w[2] * u_pad[:, 2:]
    conv_new = u_pad[:, -(CONV_K - 1):]
    a_out = _rmsnorm((bg * y).reshape(bsz, T, CONV_GROUPS, CONV_GROUP_DIM), g_conv).reshape(bsz, T, CONV_W)
    li = ip + b_igate
    lf = jax.nn.log_sigmoid((fp + b_fgate).astype(jnp.float32))
    hm, C, n, m = _mlstm(q.reshape(bsz, T, M_HEADS, M_DK), k.reshape(bsz, T, M_HEADS, M_DK),
                         v.reshape(bsz, T, M_HEADS, M_DV), li, lf, C0, n0, m0)
    hm = _rmsnorm(hm.astype(h.dtype), g_mlstm) * jax.nn.sigmoid(o).reshape(bsz, T, M_HEADS, M_DV)
    mix = jnp.concatenate([a_out, hm.reshape(bsz, T, M_HEADS * M_DV)], axis=-1)
    return mix @ w_out, conv_new, C, n, m

def _trunk(x, conv0, C0, n0, m0, ffn1_norm, ffn1_w_gate, ffn1_w_up, ffn1_w_down, mix_norm, w_in,
           b_igate, b_fgate, conv_w, conv_b, g_conv, g_mlstm, w_out, ffn2_norm, ffn2_w_gate,
           ffn2_w_up, ffn2_w_down, final_norm):
    convs, Cs, ns, ms = [], [], [], []
    for l in range(DEPTH):
        x = x + 0.5 * _swiglu(_rmsnorm(x, ffn1_norm[l]), ffn1_w_gate[l], ffn1_w_up[l], ffn1_w_down[l])
        y, cv, C, n, m = _mixer(_rmsnorm(x, mix_norm[l]), conv0[l], C0[l], n0[l], m0[l], w_in[l],
                                b_igate[l], b_fgate[l], conv_w[l], conv_b[l], g_conv[l], g_mlstm[l], w_out[l])
        x = x + y
        x = x + 0.5 * _swiglu(_rmsnorm(x, ffn2_norm[l]), ffn2_w_gate[l], ffn2_w_up[l], ffn2_w_down[l])
        convs.append(cv)
        Cs.append(C)
        ns.append(n)
        ms.append(m)
    return _rmsnorm(x, final_norm), jnp.stack(convs), jnp.stack(Cs), jnp.stack(ns), jnp.stack(ms)

def setup_inputs(seed: int = 0) -> dict:
    key = jax.random.key(seed)
    ks = jax.random.split(key, 32)
    nrm = lambda k, shape, s: jax.random.normal(k, shape, jnp.float32) * s
    gain = lambda k, shape: 1.0 + 0.05 * jax.random.normal(k, shape, jnp.float32)
    b_f = jnp.linspace(3.0, 6.0, M_HEADS, dtype=jnp.float32)[None, :] + nrm(ks[13], (DEPTH, M_HEADS), 0.1)
    return {
        'x_prompt': nrm(ks[0], (BATCH, SEQ, D_MODEL), 1.0),
        'x_sample': nrm(ks[1], (DEC_BATCH, DEC_SEQ, D_MODEL), 1.0),
        'cache_conv': nrm(ks[2], (DEPTH, DEC_BATCH, CONV_K - 1, CONV_W), 1.0),
        'state_C': nrm(ks[3], (DEPTH, DEC_BATCH, M_HEADS, M_DK, M_DV), 0.1),
        'state_n': jnp.abs(nrm(ks[4], (DEPTH, DEC_BATCH, M_HEADS, M_DK), 0.5)),
        'state_m': nrm(ks[5], (DEPTH, DEC_BATCH, M_HEADS), 0.5),
        'ffn1_norm': gain(ks[6], (DEPTH, D_MODEL)),
        'ffn1_w_gate': nrm(ks[7], (DEPTH, D_MODEL, D_FF), D_MODEL ** -0.5),
        'ffn1_w_up': nrm(ks[8], (DEPTH, D_MODEL, D_FF), D_MODEL ** -0.5),
        'ffn1_w_down': nrm(ks[9], (DEPTH, D_FF, D_MODEL), D_FF ** -0.5),
        'mix_norm': gain(ks[10], (DEPTH, D_MODEL)),
        'w_in': nrm(ks[11], (DEPTH, D_MODEL, N_IN), D_MODEL ** -0.5),
        'b_igate': nrm(ks[12], (DEPTH, M_HEADS), 0.1),
        'b_fgate': b_f,
        'conv_w': nrm(ks[14], (DEPTH, CONV_K, CONV_W), 0.5),
        'conv_b': nrm(ks[15], (DEPTH, CONV_W), 0.01),
        'g_conv': gain(ks[16], (DEPTH, CONV_GROUPS, CONV_GROUP_DIM)),
        'g_mlstm': gain(ks[17], (DEPTH, M_HEADS, M_DV)),
        'w_out': nrm(ks[18], (DEPTH, D_MIX, D_MODEL), D_MIX ** -0.5),
        'ffn2_norm': gain(ks[19], (DEPTH, D_MODEL)),
        'ffn2_w_gate': nrm(ks[20], (DEPTH, D_MODEL, D_FF), D_MODEL ** -0.5),
        'ffn2_w_up': nrm(ks[21], (DEPTH, D_MODEL, D_FF), D_MODEL ** -0.5),
        'ffn2_w_down': nrm(ks[22], (DEPTH, D_FF, D_MODEL), D_FF ** -0.5),
        'final_norm': gain(ks[23], (D_MODEL,)),
    }

def reference(x_prompt, x_sample, cache_conv, state_C, state_n, state_m, ffn1_norm, ffn1_w_gate,
              ffn1_w_up, ffn1_w_down, mix_norm, w_in, b_igate, b_fgate, conv_w, conv_b, g_conv,
              g_mlstm, w_out, ffn2_norm, ffn2_w_gate, ffn2_w_up, ffn2_w_down, final_norm):
    bsz = x_prompt.shape[0]
    conv0 = jnp.zeros((DEPTH, bsz, CONV_K - 1, CONV_W), x_prompt.dtype)
    C0 = jnp.zeros((DEPTH, bsz, M_HEADS, M_DK, M_DV), jnp.float32)
    n0 = jnp.zeros((DEPTH, bsz, M_HEADS, M_DK), jnp.float32)
    m0 = jnp.zeros((DEPTH, bsz, M_HEADS), jnp.float32)
    y_prompt, p_conv, p_C, p_n, p_m = _trunk(
        x_prompt, conv0, C0, n0, m0, ffn1_norm, ffn1_w_gate, ffn1_w_up, ffn1_w_down, mix_norm, w_in,
        b_igate, b_fgate, conv_w, conv_b, g_conv, g_mlstm, w_out, ffn2_norm, ffn2_w_gate, ffn2_w_up,
        ffn2_w_down, final_norm)
    y_sample, s_conv, s_C, s_n, s_m = _trunk(
        x_sample, cache_conv, state_C, state_n, state_m, ffn1_norm, ffn1_w_gate, ffn1_w_up, ffn1_w_down,
        mix_norm, w_in, b_igate, b_fgate, conv_w, conv_b, g_conv, g_mlstm, w_out, ffn2_norm, ffn2_w_gate,
        ffn2_w_up, ffn2_w_down, final_norm)
    return (y_prompt, y_sample, p_conv, p_C, p_n, p_m, s_conv, s_C, s_n, s_m)


_drawn_inputs = setup_inputs


def setup_inputs(seed=0):
    import zlib

    import numpy as np

    out = dict(_drawn_inputs(seed))
    spreads = {}
    factors = {'state_C': 3.776, 'state_m': 3.798, 'conv_b': 7.932, 'g_mlstm': 3.979, 'ffn2_norm': 3.574}
    for name, (base, spread) in spreads.items():
        noise = np.random.default_rng([zlib.crc32(name.encode()), seed]).standard_normal(out[name].shape)
        drawn = base * np.exp(spread * noise) if base else spread * noise
        out[name] = __import__('jax').numpy.asarray(drawn.astype(out[name].dtype))
    for name, factor in factors.items():
        out[name] = (out[name] * factor).astype(out[name].dtype)
    return out
```

```python
import numpy as np
import concourse.bass as bass
from concourse import mybir
from contextlib import ExitStack

FP32 = mybir.dt.float32
FP32R = mybir.dt.float32r
BF16 = mybir.dt.bfloat16
ALU = mybir.AluOpType
ACT = mybir.ActivationFunctionType

D_MODEL = 1024
SEQ = 1024
DEC_SEQ = 32
TOKENS = SEQ + DEC_SEQ
P = 128
KT = D_MODEL // P
D_FF = ((8 * D_MODEL // 3 + 127) // 128) * 128
FT = D_FF // P
BLOCKS = 3
BLK = TOKENS // BLOCKS
CONV_W = D_MODEL // 2
CT = CONV_W // P
HEADS = 4
PAIRS = HEADS // 2
DV = (D_MODEL - CONV_W) // HEADS
DK = DV // 2
CHUNK = 128
CHUNKS = SEQ // CHUNK
EPS = 1e-6
N_IN = 3 * CONV_W + 2 * HEADS * DK + 2 * HEADS * DV + 2 * HEADS
COL_Q = 3 * CONV_W
COL_GATES = N_IN - 2 * HEADS
NEG = -1e30

V_FFN1, V_MIX, V_FFN2, V_FINAL, V_CONVW, V_CONVB, V_GCONV, V_GMLSTM, V_CACHE, V_END = (
    0, 8, 16, 24, 32, 44, 48, 52, 56, 64)


NORM_FFN1, NORM_MIX, NORM_FFN2, NORM_FINAL = range(0, 4 * BLOCKS, BLOCKS)


def block_columns(b):
    return slice(b * BLK, (b + 1) * BLK)


class Shared:
    pass



def norm_semaphores(sh):
    sh.squared = sh.sem("squared")
    sh.square_added = sh.sem("square_added")
    sh.stats_done = sh.sem("stats_done")
    sh.root_step = sh.sem("root_step")
    sh.reciprocal_ready = sh.sem("reciprocal_ready")
    sh.root_ready = sh.sem("root_ready")
    sh.scaled = sh.sem("scaled")
    sh.norm_high = sh.sem("norm_high")
    sh.norm_low = sh.sem("norm_low")


def norm_buffers(sb):
    norm = Shared()
    norm.square = sb("square", [P, 2, BLK], FP32)
    norm.square_sum = sb("square_sum", [P, BLK], FP32)
    norm.mean_square = sb("mean_square", [P, BLK], FP32)
    norm.root_work = sb("root_work", [P, BLK], FP32)
    norm.inv_rms = sb("inv_rms", [P, BLK], FP32)
    norm.normed = sb("normed", [P, 3, BLK], FP32)
    return norm


def norm_square(act, sh, n, k):
    i = (n - 1) * KT + k
    if i >= 2:
        act.wait_ge(sh.square_added, i - 1)
    act.activation(sh.norm.square[:, i % 2, :], sh.x[:, k, block_columns(n % BLOCKS)],
                   ACT.Square).then_inc(sh.squared, 1)


def norm_squares(act, sh, n, ready, before):
    for k in range(KT):
        act.wait_ge(ready, before + k + 1)
        norm_square(act, sh, n, k)


def norm_add(pool, sh, n):
    if n >= 2:
        pool.wait_ge(sh.stats_done, n)
    for k in range(KT):
        i = (n - 1) * KT + k
        pool.wait_ge(sh.squared, i + 1)
        if i:
            pool.wait_ge(sh.square_added, i)
        if k:
            pool.tensor_tensor(sh.norm.square_sum[:, :], sh.norm.square_sum[:, :], sh.norm.square[:, i % 2, :],
                               ALU.add).then_inc(sh.square_added, 1)
        else:
            pool.tensor_copy(sh.norm.square_sum[:, :], sh.norm.square[:, i % 2, :]).then_inc(sh.square_added, 1)


def norm_stats(pe, sh, n, bank):
    pe.wait_ge(sh.square_added, n * KT)
    pe.wait_ge(sh.root_step, 4 * (n - 1) + 1)
    pe.matmul(bank[:, 0:BLK], sh.mean_all[:, :], sh.norm.square_sum[:, :],
              start=True, stop=True).then_inc(sh.stats_done, 1)


def norm_root_dve(dve, sh, n, bank):
    mean, root, work = sh.norm.mean_square[:, :], sh.norm.inv_rms[:, :], sh.norm.root_work[:, :]
    dve.wait_ge(sh.stats_done, n + 1)
    if n >= 1:
        dve.wait_ge(sh.scaled, KT * n)
        dve.wait_ge(sh.root_step, 4 * n)
    dve.tensor_scalar(mean, bank[:, 0:BLK], EPS, None, ALU.add).then_inc(sh.root_step, 1)
    dve.wait_ge(sh.root_step, 4 * n + 1)
    dve.reciprocal(work, mean).then_inc(sh.reciprocal_ready, 1)
    dve.wait_ge(sh.root_ready, n + 1)
    dve.tensor_tensor(work, root, root, ALU.mult).then_inc(sh.root_step, 1)
    dve.wait_ge(sh.root_step, 4 * n + 2)
    dve.scalar_tensor_tensor(work, work, -0.5, mean, ALU.mult, ALU.mult).then_inc(sh.root_step, 1)
    dve.wait_ge(sh.root_step, 4 * n + 3)
    dve.scalar_tensor_tensor(root, work, 1.5, root, ALU.add, ALU.mult).then_inc(sh.root_step, 1)
    dve.wait_ge(sh.root_step, 4 * n + 4)


def norm_root_act(act, sh, n):
    act.wait_ge(sh.reciprocal_ready, n + 1)
    act.activation(sh.norm.inv_rms[:, :], sh.norm.root_work[:, :], ACT.Sqrt).then_inc(sh.root_ready, 1)


def norm_split_dve(dve, sh, n, gain):
    def low(i):
        dve.wait_ge(sh.norm_high, i + 1)
        dve.tensor_tensor(sh.in_lo[:, i % KT, block_columns(n % BLOCKS)], sh.norm.normed[:, i % 3, :],
                          sh.in_hi[:, i % KT, block_columns(n % BLOCKS)].bitcast(FP32), ALU.subtract
                          ).then_inc(sh.norm_low, 1)

    for k in range(KT):
        i = n * KT + k
        if i >= 3:
            dve.wait_ge(sh.norm_low, i - 2)
        dve.scalar_tensor_tensor(sh.norm.normed[:, i % 3, :], sh.x[:, k, block_columns(n % BLOCKS)],
                                 sh.vectors[:, gain + k:gain + k + 1], sh.norm.inv_rms[:, :],
                                 ALU.mult, ALU.mult).then_inc(sh.scaled, 1)
        if k:
            low(i - 1)
    low(n * KT + KT - 1)


def norm_split_act(act, sh, n, also=None):
    for k in range(KT):
        i = n * KT + k
        if also is not None:
            also(k)
        act.wait_ge(sh.scaled, i + 1)
        act.activation(sh.in_hi[:, k, block_columns(n % BLOCKS)], sh.norm.normed[:, i % 3, :], ACT.Copy
                       ).then_inc(sh.norm_high, 1)


def norm_scale(dve, sh, n, gain):
    for k in range(KT):
        x = sh.x[:, k, block_columns(n % BLOCKS)]
        dve.scalar_tensor_tensor(x, x, sh.vectors[:, gain + k:gain + k + 1], sh.norm.inv_rms[:, :],
                                 ALU.mult, ALU.mult).then_inc(sh.scaled, 1)


def norm_dve(dve, sh, n, bank, gain):
    norm_root_dve(dve, sh, n, bank)
    if n >= NORM_FINAL:
        norm_scale(dve, sh, n, gain)
    else:
        norm_split_dve(dve, sh, n, gain)


def norm_act(act, sh, n, also=None):
    norm_root_act(act, sh, n)
    if n < NORM_FINAL:
        norm_split_act(act, sh, n, also)


def products(pe, out, w_hi, w_lo, in_hi, in_lo, first=True, last=True):
    pe.matmul(out, w_hi, in_hi, start=first, stop=False)
    pe.matmul(out, w_hi, in_lo, start=False, stop=False)
    return pe.matmul(out, w_lo, in_hi, start=False, stop=last)


KINDS = ("gate", "up", "down")
SLOT = {("gate", 0): 0, ("up", 0): 1, ("gate", 1): 2, ("up", 1): 3, ("down", 0): 4, ("down", 1): 5}
FIRST_TILES = (("gate", 0), ("up", 0), ("gate", 1), ("up", 1), ("down", 0), ("down", 1))


def wide_buffers(sh, sb):
    norm = norm_buffers(sb)
    for a, kind in ((sh.raw, "raw"), (sh.w_hi, "w_hi"), (sh.w_lo, "w_lo")):
        more = sb(f"{kind}_more", [P, 3, D_MODEL], FP32 if kind == "raw" else FP32R)
        del a[3:]
        a.extend(more[:, i, :] for i in range(3))
    return norm


def ffn_weights(sh, name, w_gate, w_up, w_down):
    f = Shared()
    f.view = {"gate": w_gate.rearrange("(k p) n -> p k n", p=P), "up": w_up.rearrange("(k p) n -> p k n", p=P),
              "down": w_down.rearrange("(f p) n -> p f n", p=P)}
    f.loaded = {w: [sh.sem(f"{name}_{w}_loaded{j}") for j in range(2)] for w in KINDS}
    f.high = {w: sh.sem(f"{name}_{w}_high") for w in KINDS}
    f.low = {w: sh.sem(f"{name}_{w}_low") for w in KINDS}
    return f


def weight_load(sp, sh, f, w, tile, j):
    dst = sh.raw[SLOT[w, j]]
    if w == "down":
        src = f.view[w][:, bass.ds(tile, 1), :].rearrange("p f n -> p (f n)")
        sp.dma_start(dst, src).then_inc(f.loaded[w][j], 16)
    else:
        sp.dma_start(dst.rearrange("p (k n) -> p k n", n=P),
                     f.view[w][:, :, bass.ds(tile * P, P)]).then_inc(f.loaded[w][j], 16)


def weight_high(act, sh, f, w, j, pair):
    act.wait_ge(f.loaded[w][j], pair * 16 + 16)
    act.activation(sh.w_hi[SLOT[w, j]], sh.raw[SLOT[w, j]], ACT.Copy).then_inc(f.high[w], 1)


def weight_low(dve, sh, f, w, j, pair):
    dve.wait_ge(f.high[w], pair * 2 + j + 1)
    dve.tensor_tensor(sh.w_lo[SLOT[w, j]], sh.raw[SLOT[w, j]], sh.w_hi[SLOT[w, j]].bitcast(FP32),
                      ALU.subtract).then_inc(f.low[w], 1)


def hidden_buffers(nc, name, ctx):
    return [ctx.enter_context(nc.sbuf_tensor(f"{name}_{n}", [P, 2, BLK], dt))
            for n, dt in (("silu", FP32), ("hidden", FP32), ("hidden_hi", FP32R), ("hidden_lo", FP32R))]


def ffn_phase(nc, sh, name, f, own_norms, gain, out_norm, out_gain, following=None, hidden_tensors=None):
    with ExitStack() as ctx:
        silu, hidden, h_hi, h_lo = hidden_tensors or hidden_buffers(nc, name, ctx)
        gate_bank, up_bank, down_bank = sh.bank[0:2], sh.bank[2:4], sh.bank[4:8]
        s = Shared()
        s.gate_done = sh.sem(f"{name}_gate_done")
        s.up_done = sh.sem(f"{name}_up_done")
        s.silu_ready = sh.sem(f"{name}_silu_ready")
        s.hidden_ready = sh.sem(f"{name}_hidden_ready")
        s.hidden_high = sh.sem(f"{name}_hidden_high")
        s.hidden_low = sh.sem(f"{name}_hidden_low")
        s.down_done = sh.sem(f"{name}_down_done")
        s.x_added = sh.sem(f"{name}_x_added")
        sh.x_added = s.x_added
        block = sh.block
        PAIRS_F = FT // 2
        ROUNDS = PAIRS_F * BLOCKS

        def loop(engine, body):
            body(0, True, False)
            with engine.Fori(1, PAIRS_F - 1) as pair:
                body(pair, False, False)
            body(PAIRS_F - 1, False, True)

        @block.sync
        def _(sp):
            with sp.Fori(1, PAIRS_F) as pair:
                for w, j in FIRST_TILES:
                    sp.wait_ge(f.low[w], pair * 2 + (j - 1))
                    weight_load(sp, sh, f, w, pair * 2 + j, j)
            if following:
                following.loads(sp)

        @block.gpsimd
        def _(pool):
            if following:
                following.clears(pool)
            for b in range(BLOCKS):
                norm_add(pool, sh, out_norm + b)

        @block.scalar
        def _(act):
            def hidden_of(r, j):
                step = r * 2 + j
                act.wait_ge(s.gate_done, step + 1)
                if not (isinstance(r, int) and r == 0):
                    act.wait_ge(s.hidden_ready, step - 1)
                act.activation(silu[:, j, :], gate_bank[j][:, 0:BLK], ACT.Silu).then_inc(s.silu_ready, 1)
                act.wait_ge(s.hidden_ready, step + 1)
                if not (isinstance(r, int) and r == 0):
                    act.wait_ge(s.down_done, r * 8)
                act.activation(h_hi[:, j, :], hidden[:, j, :], ACT.Copy).then_inc(s.hidden_high, 1)

            def body(pair, first, last):
                for b in range(BLOCKS):
                    r = pair * 3 + b
                    if b == 0 and not first:
                        act.wait_ge(s.up_done, r * 2)
                        weight_high(act, sh, f, "gate", 1, pair)
                        weight_high(act, sh, f, "up", 1, pair)
                        act.wait_ge(s.down_done, r * 8)
                        weight_high(act, sh, f, "down", 0, pair)
                        weight_high(act, sh, f, "down", 1, pair)
                    if last and b:
                        norm_squares(act, sh, out_norm + b - 1, s.x_added, (r - 1) * 8)
                    if last and b == 2:
                        norm_act(act, sh, out_norm)
                    if first and b < len(own_norms) == 2:
                        norm_act(act, sh, own_norms[b],
                                 None if b else lambda k: norm_square(act, sh, own_norms[1], k))
                    hidden_of(r, 0)
                    if b == 2 and not last:
                        act.wait_ge(s.up_done, r * 2 + 1)
                        weight_high(act, sh, f, "gate", 0, pair + 1)
                        weight_high(act, sh, f, "up", 0, pair + 1)
                    if following and last and b == 2:
                        act.wait_ge(s.up_done, r * 2 + 1)
                        following.early_high(act)
                    hidden_of(r, 1)
                    if first and b == 0 and len(own_norms) == 1:
                        norm_act(act, sh, own_norms[0])

            loop(act, body)
            if following:
                act.wait_ge(s.up_done, ROUNDS * 2)
                following.late_high(act)
            norm_squares(act, sh, out_norm + 2, s.x_added, (ROUNDS - 1) * 8)
            norm_act(act, sh, out_norm + 1)

        @block.vector
        def _(dve):
            def hidden_of(r, j):
                step = r * 2 + j
                dve.wait_ge(s.silu_ready, step + 1)
                dve.wait_ge(s.up_done, step + 1)
                if not (isinstance(r, int) and r == 0):
                    dve.wait_ge(s.hidden_low, step - 1)
                dve.tensor_tensor(hidden[:, j, :], silu[:, j, :], up_bank[j][:, 0:BLK], ALU.mult
                                  ).then_inc(s.hidden_ready, 1)
                dve.wait_ge(s.hidden_high, step + 1)
                dve.tensor_tensor(h_lo[:, j, :], hidden[:, j, :], h_hi[:, j, :].bitcast(FP32),
                                  ALU.subtract).then_inc(s.hidden_low, 1)

            def add_down(r, b):
                if not (isinstance(r, int) and r < 3):
                    dve.wait_ge(s.x_added, r * 8 - 16)
                for d in range(KT):
                    dve.wait_ge(s.down_done, r * 8 + (d + 1))
                    dve.scalar_tensor_tensor(sh.x[:, d, block_columns(b)], down_bank[d % 4][:, 0:BLK], 0.5,
                                             sh.x[:, d, block_columns(b)], ALU.mult, ALU.add
                                             ).then_inc(s.x_added, 1)

            def body(pair, first, last):
                for b in range(BLOCKS):
                    r = pair * 3 + b
                    if b == 0 and not first:
                        weight_low(dve, sh, f, "gate", 1, pair)
                        weight_low(dve, sh, f, "up", 1, pair)
                        weight_low(dve, sh, f, "down", 0, pair)
                        weight_low(dve, sh, f, "down", 1, pair)
                    if last and b == 2:
                        norm_dve(dve, sh, out_norm, gate_bank[0], out_gain)
                    if first and b < len(own_norms) == 2:
                        norm_dve(dve, sh, own_norms[b], down_bank[3], gain)
                    hidden_of(r, 0)
                    if b == 2 and not last:
                        weight_low(dve, sh, f, "gate", 0, pair + 1)
                        weight_low(dve, sh, f, "up", 0, pair + 1)
                    if following and last and b == 2:
                        following.early_low(dve)
                    hidden_of(r, 1)
                    if first and b == 0 and len(own_norms) == 1:
                        norm_dve(dve, sh, own_norms[0], down_bank[3], gain)
                    add_down(r, b)

            loop(dve, body)
            if following:
                following.late_low(dve)
            norm_dve(dve, sh, out_norm + 1, gate_bank[0], out_gain)

        @block.tensor
        def _(pe):
            def gate_up(pair, r, b, j, first, last):
                step = r * 2 + j
                for w, bank, read in (("gate", gate_bank[j], s.silu_ready), ("up", up_bank[j], s.hidden_ready)):
                    if not (isinstance(r, int) and r == 0):
                        pe.wait_ge(read, step - 1)
                    if first and len(own_norms) == 2 and (b, j, w) == (0, 0, "up"):
                        for copied in sh.tokens_copied:
                            pe.wait_ge(copied, SEQ // P + 1)
                    if first and (b, j, w) == ((0, 0, "up") if len(own_norms) == 2 else (0, 1, "gate")):
                        norm_stats(pe, sh, own_norms[0], down_bank[3])
                    if first and len(own_norms) == 2 and (b, j, w) == (1, 0, "gate"):
                        pe.wait_ge(s.x_added, KT)
                        norm_stats(pe, sh, own_norms[1], down_bank[3])
                    if last and b == 2 and j == 0 and w == "gate":
                        pe.wait_ge(sh.root_step, out_norm * 4 + 1)
                    if b == 0:
                        pe.wait_ge(f.low[w], pair * 2 + (j + 1))
                    for k in range(KT):
                        if first and j == 0 and w == "gate":
                            pe.wait_ge(sh.norm_low, (own_norms[-1] - 2 + b) * KT + k + 1)
                        col = slice(k * P, (k + 1) * P)
                        done = products(pe, bank[:, 0:BLK], sh.w_hi[SLOT[w, j]][:, col], sh.w_lo[SLOT[w, j]][:, col],
                                        sh.in_hi[:, k, block_columns(b)], sh.in_lo[:, k, block_columns(b)],
                                        k == 0, k == KT - 1)
                    done.then_inc(s.gate_done if w == "gate" else s.up_done, 1)

            def down(pair, r, b):
                def half(d, j):
                    col = slice(d * P, (d + 1) * P)
                    return products(pe, down_bank[d % 4][:, 0:BLK], sh.w_hi[SLOT["down", j]][:, col],
                                    sh.w_lo[SLOT["down", j]][:, col], h_hi[:, j, :], h_lo[:, j, :], j == 0, j == 1)

                for j in range(2):
                    pe.wait_ge(s.hidden_low, r * 2 + (j + 1))
                    if b == 0:
                        pe.wait_ge(f.low["down"], pair * 2 + (j + 1))
                    for d in range(4):
                        if j == 0 and not (isinstance(r, int) and r == 0):
                            pe.wait_ge(s.x_added, r * 8 + (d - 3))
                        done = half(d, j)
                        if j == 1:
                            done.then_inc(s.down_done, 1)
                for d in range(4, KT):
                    pe.wait_ge(s.x_added, r * 8 + (d - 3))
                    half(d, 0)
                    half(d, 1).then_inc(s.down_done, 1)

            def body(pair, first, last):
                for b in range(BLOCKS):
                    r = pair * 3 + b
                    gate_up(pair, r, b, 0, first, last)
                    gate_up(pair, r, b, 1, first, last)
                    if first and b < len(own_norms):
                        pe.wait_ge(sh.root_step, own_norms[b] * 4 + 1)
                    if last and b:
                        pe.wait_ge(s.silu_ready, r * 2 + 1)
                        norm_stats(pe, sh, out_norm + b - 1, gate_bank[0])
                    down(pair, r, b)

            loop(pe, body)


def load_phase(nc, sh, x_prompt, x_sample, vector_rows, f):
    with ExitStack() as ctx:
        tokens = ctx.enter_context(nc.sbuf_tensor("tokens", [P, 3, D_MODEL], FP32))
        rows = ctx.enter_context(nc.sbuf_tensor("vector_rows", [V_END, P], FP32))
        pairs = [(sh.bank[a], sh.bank[b]) for a, b in ((4, 5), (6, 7), (1, 3))]
        vec_bank, stats_bank = sh.bank[2], sh.bank[0]
        const = sh.sem("const")
        vec_in = sh.sem("vec_in")
        vec_t = sh.sem("vec_t")
        vec_out = sh.sem("vec_out")
        buffers = [*(tokens[:, i, :] for i in range(3)), *sh.raw[2:6]]
        TURN = len(buffers)
        tok_in = [sh.sem(f"tok_in{i}") for i in range(TURN)]
        first_squared = sh.sem("first_squared")
        transposed = sh.sem("tokens_transposed")
        copied_dve = sh.sem("tokens_copied_dve")
        copied_act = sh.sem("tokens_copied_act")
        sh.tokens_copied = (copied_dve, copied_act)
        block = sh.block
        TILES = SEQ // P + 1
        count = [P] * (SEQ // P) + [DEC_SEQ]

        def first_square(k):
            return sh.x[:, KT + k % 4, block_columns(k // 4)]

        @block.sync
        def _(sp):
            for view, first in vector_rows:
                sp.dma_start(rows[first:first + view.shape[0], :], view).then_inc(vec_in, 16)
            for t, n in enumerate(count):
                if t >= TURN:
                    sp.wait_ge(transposed, t - TURN + 1)
                src = x_prompt[t * P:(t + 1) * P, :] if t < SEQ // P else x_sample
                sp.dma_start(buffers[t % TURN][0:n, :], src).then_inc(tok_in[t % TURN], 16)
                if t == 2:
                    for w, j in FIRST_TILES[:2]:
                        weight_load(sp, sh, f, w, j, j)
            for i, (w, j) in enumerate(FIRST_TILES[2:]):
                sp.wait_ge(transposed, 3 + i + 1)
                weight_load(sp, sh, f, w, j, j)

        @block.gpsimd
        def _(pool):
            n = 0
            for tile, value in ((sh.ident, 0.0), (sh.mask, 0.0), (sh.ident16, 0.0), (sh.head_row, 0.0),
                                (sh.pair_rows, 0.0), (sh.mean_all, 1.0 / D_MODEL), (sh.mean_group, 0.0)):
                pool.memset(tile[:], value).then_inc(const, 1)
                n += 1
                pool.wait_ge(const, n)
            for m in (sh.ident, sh.ident16):
                pool.affine_select(out=m[:, :], in_=m[:, :], compare_op=ALU.not_equal, fill=1.0, base=0,
                                   pattern=[[-1, P]], channel_multiplier=1).then_inc(const, 1)
            pool.affine_select(out=sh.mask[:, :], in_=sh.mask[:, :], compare_op=ALU.is_ge, fill=NEG,
                               base=0, pattern=[[1, P]], channel_multiplier=-1).then_inc(const, 1)
            pool.affine_select(out=sh.head_row[:], in_=sh.head_row[:], compare_op=ALU.not_equal,
                               fill=-1.0, base=0, pattern=[[1, HEADS], [0, P]], channel_multiplier=-1
                               ).then_inc(const, 1)
            pool.affine_select(out=sh.pair_rows[:].rearrange("r p (e d) -> r p e d", e=2),
                               in_=sh.pair_rows[:].rearrange("r p (e d) -> r p e d", e=2),
                               compare_op=ALU.not_equal, fill=DK ** -0.5, base=0,
                               pattern=[[2, PAIRS], [1, 2], [0, DK]], channel_multiplier=-1
                               ).then_inc(const, 1)
            pool.wait_ge(const, n + 5)
            for e in range(2):
                g = slice(e * DK, (e + 1) * DK)
                pool.memset(sh.mean_group[g, g], 1.0 / DK).then_inc(const, 1)
                n += 1
                pool.wait_ge(const, n + 5)
            for b in range(1, BLOCKS):
                norm_add(pool, sh, b)

        @block.tensor
        def _(pe):
            def tile(t):
                n = count[t]
                pe.wait_ge(tok_in[t % TURN], 16 * (t // TURN) + 16)
                if t >= 3:
                    pe.wait_ge(copied_dve, t - 2)
                    pe.wait_ge(copied_act, t - 2)
                for k in range(KT):
                    last = pe.transpose(pairs[t % 3][k // 4][:, (k % 4) * P:(k % 4) * P + n],
                                        buffers[t % TURN][0:n, k * P:(k + 1) * P], sh.ident[0:n, 0:n])
                last.then_inc(transposed, 1)

            pe.wait_ge(const, 14)
            pe.wait_ge(vec_in, 16 * len(vector_rows))
            pe.transpose(vec_bank[:, 0:V_END], rows[:, :], sh.ident[0:V_END, 0:V_END]).then_inc(vec_t, 1)
            for t in range(3):
                tile(t)
            for k in range(KT):
                pe.wait_ge(first_squared, k + 1)
                last = pe.matmul(stats_bank[:, 0:BLK], sh.mean_all[:, :], first_square(k),
                                 start=k == 0, stop=k == KT - 1)
            last.then_inc(sh.stats_done, 1)
            for t in range(3, TILES):
                tile(t)
            pe.wait_ge(vec_out, 1)
            pe.wait_ge(sh.root_step, 1)

        @block.vector
        def _(dve):
            def tile(t):
                dve.wait_ge(transposed, t + 1)
                dve.tensor_copy(sh.x[:, 0:4, t * P:t * P + count[t]],
                                pairs[t % 3][0][:, :].rearrange("p (k n) -> p k n", n=P)[:, :, 0:count[t]]
                                ).then_inc(copied_dve, 1)

            dve.wait_ge(vec_t, 1)
            dve.tensor_copy(sh.vectors[:, :], vec_bank[:, 0:V_END]).then_inc(vec_out, 1)
            for t in range(3):
                tile(t)
            weight_low(dve, sh, f, "gate", 0, 0)
            weight_low(dve, sh, f, "up", 0, 0)
            for t in range(3, 6):
                tile(t)
            dve.wait_ge(vec_out, 1)
            norm_dve(dve, sh, 0, stats_bank, V_FFN1)
            for t in range(6, TILES):
                tile(t)
            weight_low(dve, sh, f, "gate", 1, 0)
            weight_low(dve, sh, f, "up", 1, 0)
            weight_low(dve, sh, f, "down", 0, 0)
            weight_low(dve, sh, f, "down", 1, 0)

        @block.scalar
        def _(act):
            def tile(t):
                act.wait_ge(transposed, t + 1)
                act.activation(sh.x[:, 4:8, t * P:t * P + count[t]],
                               pairs[t % 3][1][:, :].rearrange("p (k n) -> p k n", n=P)[:, :, 0:count[t]],
                               ACT.Copy).then_inc(copied_act, 1)

            for t in range(3):
                tile(t)
            act.wait_ge(copied_dve, 3)
            act.wait_ge(copied_act, 3)
            for k in range(KT):
                act.activation(first_square(k), sh.x[:, k, block_columns(0)], ACT.Square).then_inc(first_squared, 1)
            weight_high(act, sh, f, "gate", 0, 0)
            weight_high(act, sh, f, "up", 0, 0)
            for t in range(3, 6):
                tile(t)
            act.wait_ge(copied_dve, 6)
            act.wait_ge(copied_act, 6)
            norm_act(act, sh, 0, lambda k: norm_square(act, sh, 1, k))
            for t in range(6, TILES):
                tile(t)
            weight_high(act, sh, f, "gate", 1, 0)
            weight_high(act, sh, f, "up", 1, 0)
            weight_high(act, sh, f, "down", 0, 0)
            weight_high(act, sh, f, "down", 1, 0)
            act.wait_ge(copied_dve, TILES)
            act.wait_ge(copied_act, TILES)


def final_phase(nc, sh, y_prompt, y_sample):
    TILES = SEQ // P + 1
    pairs = [sh.bank[0:2], sh.bank[2:4], sh.bank[4:6]]
    out = sh.raw
    transposed = sh.sem("y_transposed")
    copied_dve = sh.sem("y_copied_dve")
    copied_act = sh.sem("y_copied_act")
    stored = [sh.sem(f"y_stored{i}") for i in range(4)]
    count = [P] * (SEQ // P) + [DEC_SEQ]
    BEFORE = 5
    block = sh.block

    @block.scalar
    def _(act):
        for t, n in enumerate(count):
            if t == BEFORE:
                norm_act(act, sh, NORM_FINAL + 2)
            act.wait_ge(transposed, t + 1)
            if t >= 4:
                act.wait_ge(stored[t % 4], 16 * (t // 4))
            act.activation(out[t % 4][0:n, 512:1024], pairs[t % 3][1][0:n, :], ACT.Copy).then_inc(copied_act, 1)

    @block.vector
    def _(dve):
        for t, n in enumerate(count):
            if t == BEFORE:
                norm_dve(dve, sh, NORM_FINAL + 2, sh.bank[7], V_FINAL)
            dve.wait_ge(transposed, t + 1)
            if t >= 4:
                dve.wait_ge(stored[t % 4], 16 * (t // 4))
            dve.tensor_copy(out[t % 4][0:n, 0:512], pairs[t % 3][0][0:n, :]).then_inc(copied_dve, 1)

    @block.tensor
    def _(pe):
        pe.wait_ge(sh.root_step, 4 * (NORM_FINAL + 1) + 1)
        for t, n in enumerate(count):
            pe.wait_ge(sh.scaled, KT * (NORM_FINAL + (t * P + n - 1) // BLK + 1))
            if t >= 3:
                pe.wait_ge(copied_dve, t - 2)
                pe.wait_ge(copied_act, t - 2)
            for k in range(KT):
                last = pe.transpose(pairs[t % 3][k // 4][0:n, (k % 4) * P:(k % 4 + 1) * P],
                                    sh.x[:, k, t * P:t * P + n], sh.ident[:, :])
            last.then_inc(transposed, 1)
            if t == 2:
                norm_stats(pe, sh, NORM_FINAL + 2, sh.bank[7])

    @block.sync
    def _(sp):
        for t, n in enumerate(count):
            sp.wait_ge(copied_dve, t + 1)
            sp.wait_ge(copied_act, t + 1)
            dst = y_prompt[t * P:(t + 1) * P, :] if t < SEQ // P else y_sample
            sp.dma_start(dst, out[t % 4][0:n, :]).then_inc(stored[t % 4], 16)
        for i in range(4):
            sp.wait_ge(stored[i], 16 * ((TILES - 1 - i) // 4 + 1))


def shared_tensors(nc, ctx):
    def sb(n, shape, dt):
        return ctx.enter_context(nc.sbuf_tensor(n, shape, dt))

    sh = Shared()
    sh.sem = lambda name: ctx.enter_context(nc.semaphore(name))
    sh.bank = [ctx.enter_context(nc.psum_tensor(f"bank{i}", [P, 512], FP32)) for i in range(8)]
    sh.x = sb("x", [P, 12, TOKENS], FP32)
    sh.in_hi = sb("in_hi", [P, KT, TOKENS], FP32R)
    sh.in_lo = sb("in_lo", [P, KT, TOKENS], FP32R)
    sh.raw_first = sb("raw", [P, 3, D_MODEL], FP32)
    sh.w_hi_first = sb("w_hi", [P, 3, D_MODEL], FP32R)
    sh.w_lo_first = sb("w_lo", [P, 3, D_MODEL], FP32R)
    sh.raw, sh.w_hi, sh.w_lo = ([a[:, i, :] for i in range(3)]
                                for a in (sh.raw_first, sh.w_hi_first, sh.w_lo_first))
    sh.vectors = sb("vectors", [P, V_END], FP32)
    sh.ident = sb("ident", [P, P], FP32)
    sh.ident16 = sb("ident16", [P, P], BF16)
    sh.mask = sb("mask", [P, P], BF16)
    sh.mean_all = sb("mean_all", [P, P], FP32)
    sh.mean_group = sb("mean_group", [P, P], FP32)
    sh.head_row = sb("head_row", [HEADS, HEADS, P], FP32)
    sh.pair_rows = sb("pair_rows", [HEADS, PAIRS, P], FP32)
    sh.gate_bias = sb("gate_bias", [36, 1], FP32)
    sh.max_before = sb("max_before", [HEADS, GROUPS], FP32)
    norm_semaphores(sh)
    return sh


def mixer_weights(sh, w_in, b_igate, b_fgate, state_m, x_parked, f):
    m = Shared()
    m.view = w_in.rearrange("(k p) n -> p k n", p=P)
    m.loaded = [sh.sem(f"mix_loaded{i}") for i in range(3)]
    m.raw_cleared = sh.sem("mix_raw_cleared")
    m.w_high = sh.sem("mix_w_high")
    m.w_low = sh.sem("mix_w_low")
    m.bias_in = sh.sem("mix_bias_in")
    m.parked = [sh.sem(f"mix_parked{b}") for b in range(BLOCKS)]

    def load(sp, slot, column):
        sp.dma_start(sh.raw[slot].rearrange("p (k n) -> p k n", n=P), m.view[:, :, bass.ds(column, P)]
                     ).then_inc(m.loaded[slot], 16)

    def high(act, slot):
        act.activation(sh.w_hi[slot], sh.raw[slot], ACT.Copy).then_inc(m.w_high, 1)

    def low(dve, slot, tile):
        dve.wait_ge(m.w_high, tile + 1)
        dve.tensor_tensor(sh.w_lo[slot], sh.raw[slot], sh.w_hi[slot].bitcast(FP32), ALU.subtract
                          ).then_inc(m.w_low, 1)

    m.load, m.high, m.low = load, high, low

    def clears(pool):
        pool.wait_ge(f.low["gate"], FT - 1)
        pool.memset(sh.raw[0], 0.0).then_inc(m.raw_cleared, 1)

    def loads(sp):
        for i, bias in enumerate((b_igate, b_fgate)):
            sp.dma_start(sh.gate_bias[32 * i:32 * i + HEADS, :], bias).then_inc(m.bias_in, 16)
        sp.dma_start(sh.max_before[:, 0:1], state_m).then_inc(m.bias_in, 16)
        sp.wait_ge(m.raw_cleared, 1)
        gates = sh.raw[0].rearrange("p (k n) -> p k n", n=P)
        for i in range(2):
            sp.dma_start(gates[:, :, 32 * i:32 * i + HEADS],
                         m.view[:, :, COL_GATES + HEADS * i:COL_GATES + HEADS * (i + 1)]).then_inc(m.loaded[0], 16)
        sp.wait_ge(f.low["up"], FT - 1)
        load(sp, 1, COL_Q)
        sp.wait_ge(f.low["gate"], FT)
        load(sp, 2, COL_Q + P)
        for b in range(BLOCKS):
            sp.wait_ge(sh.x_added, (FT // 2 * BLOCKS - BLOCKS + b + 1) * KT)
            sp.dma_start(x_parked[:, :, block_columns(b)], sh.x[:, 0:KT, block_columns(b)]).then_inc(m.parked[b], 16)

    def early_high(act):
        act.wait_ge(m.loaded[0], 32)
        high(act, 0)
        act.wait_ge(m.loaded[1], 16)
        high(act, 1)

    def late_high(act):
        act.wait_ge(m.loaded[2], 16)
        high(act, 2)

    def early_low(dve):
        low(dve, 0, 0)
        low(dve, 1, 1)

    def late_low(dve):
        low(dve, 2, 2)

    m.clears, m.loads, m.early_high, m.late_high, m.early_low, m.late_low = (
        clears, loads, early_high, late_high, early_low, late_low)
    return m


def out_weights(sh, w_out, conv_out, w_last):
    o = Shared()
    o.view = w_out.rearrange("(k p) n -> p k n", p=P)
    o.loaded = [sh.sem(f"out_loaded{i}") for i in range(3)]
    o.high = sh.sem("out_w_high")
    o.low = sh.sem("out_w_low")
    o.mix_high = sh.sem("out_mix_high")
    o.mix_low = sh.sem("out_mix_low")
    o.x_in = [sh.sem(f"out_x_in{b}") for b in range(BLOCKS)]
    o.done = sh.sem("out_done")
    o.added = sh.sem("out_added")

    def w_halves(d):
        if d < 6:
            slot = (1, 2, 0, 3, 4, 5)[d]
            return sh.w_hi[slot], sh.w_lo[slot]
        return tuple(w_last[:, 2 * (d - 6) + i, 0:D_MODEL] for i in range(2))

    def mixed(k, b):
        return conv_out[:, k, block_columns(b)] if k < CT else sh.x[:, KT + k - CT, block_columns(b)]

    order = [*range(CT - 1), *range(CT, KT), CT - 1]

    def load(sp, d):
        if d >= 3:
            sp.wait_ge(o.low, d - 2)
        sp.dma_start(sh.raw[(d + 1) % 3].rearrange("p (k n) -> p k n", n=P), o.view[:, :, d * P:(d + 1) * P]
                     ).then_inc(o.loaded[(d + 1) % 3], 16)

    def w_high(act, d):
        act.wait_ge(o.loaded[(d + 1) % 3], 16 * (d // 3) + 16)
        act.activation(w_halves(d)[0], sh.raw[(d + 1) % 3], ACT.Copy).then_inc(o.high, 1)

    def w_low(dve, d):
        dve.wait_ge(o.high, d + 1)
        hi, lo = w_halves(d)
        dve.tensor_tensor(lo, sh.raw[(d + 1) % 3], hi.bitcast(FP32), ALU.subtract).then_inc(o.low, 1)

    def mix_high(act, b, part):
        for k in (order[i] for i in part):
            act.activation(sh.in_hi[:, k, block_columns(b)], mixed(k, b), ACT.Copy).then_inc(o.mix_high, 1)

    def mix_low(dve, b, part):
        for i, k in ((i, order[i]) for i in part):
            dve.wait_ge(o.mix_high, b * KT + i + 1)
            dve.tensor_tensor(sh.in_lo[:, k, block_columns(b)], mixed(k, b),
                              sh.in_hi[:, k, block_columns(b)].bitcast(FP32), ALU.subtract).then_inc(o.mix_low, 1)

    def add(dve, b, d):
        i = b * KT + d
        dve.wait_ge(o.done, i + 1)
        x = sh.x[:, d, block_columns(b)]
        dve.tensor_tensor(x, x, sh.bank[4 + i % 4][:, 0:BLK], ALU.add).then_inc(o.added, 1)

    o.w_halves, o.load, o.w_high, o.w_low, o.mix_high_of, o.mix_low_of, o.add = (
        w_halves, load, w_high, w_low, mix_high, mix_low, add)
    return o


ROW_A, ROW_WK, ROW_M, ROW_ENM, ROW_KEEP = range(5)
CONV_C, CONV_U, CONV_Y, CONV_Z, CONV_SQ = range(5)
PADDED = TOKENS + 4
GROUPS = CHUNKS + 1
QKVO_TILES = (COL_GATES - COL_Q) // P
KINDS_COL = 3
FIRST_CONV = (QKVO_TILES + 1) * BLOCKS


def u_parts(b):
    lo, hi = b * BLK, (b + 1) * BLK
    parts = [(max(lo, start), min(hi, end), pad) for start, end, pad in ((0, SEQ, 2), (SEQ, TOKENS, 4))]
    return [(slice(a, z), slice(a + pad, z + pad), slice(a - lo, z - lo)) for a, z, pad in parts if a < z]


def mixer_phase(nc, sh, m, o, state_C, state_n, x_parked, conv_out, p_conv, p_C, p_n, p_m,
                s_conv, s_C, s_n, s_m, more_buffers):
    with ExitStack() as ctx:
        def sb(n, shape, dt=FP32):
            return ctx.enter_context(nc.sbuf_tensor(f"mix_{n}", shape, dt))

        def sem(n):
            return sh.sem(f"mix_{n}")

        rows = sb("rows", [P, 5, PADDED])
        state_p = sb("state_p", [P, PAIRS, DV + 1])
        state_s = sb("state_s", [P, PAIRS, DV + 1])
        conv_last = sb("conv_last", [P, 4, CT])
        conv_lines = sb("conv_lines", [4 * CT, P])
        m_out = sb("m_out", [HEADS, 2])
        row_max = sb("row_max", [HEADS, TOKENS])
        row_inter = sb("row_inter", [HEADS, TOKENS])
        max_before, gate_bias = sh.max_before, sh.gate_bias
        max_last = sb("max_last", [HEADS, GROUPS])
        decay_row = sb("decay_row", [HEADS, GROUPS])
        by_token = sb("by_token", [P, GROUPS * KINDS_COL * HEADS])
        decay = sb("decay", [P, PAIRS * GROUPS])
        staged_q = sb("staged_q", [P, HEADS, CHUNK])
        staged_kv = sb("staged_kv", [P, 6, CHUNK])
        values = sb("values", [P, HEADS, DV + 1])
        keys = sb("keys", [P, HEADS, DK])
        queries = sb("queries", [P, HEADS, CHUNK])
        probs = sb("probs", [P, HEADS, CHUNK])
        h_tok = sb("h_tok", [P, HEADS, DV])
        h_sq = sb("h_sq", [P, DV])
        den = sb("den", [P, HEADS])
        sq_sum = sb("sq_sum", [P, HEADS])
        h_root = sb("h_root", [P, HEADS])
        h_work = sb("h_work", [P, HEADS])
        o_gate = sb("o_gate", [P, HEADS, CHUNK])
        ctx.close()
        next_norm = more_buffers()

        root_work, mean_square, inv_rms = (rows[:, r, 0:TOKENS] for r in (CONV_U, CONV_Y, CONV_SQ))

        num_bank, dense = sh.bank[0], sh.bank[1:4]
        v_bank, k_bank, log_bank, score_bank = sh.bank[4:8]
        turn_bank = num_bank
        numerators = [num_bank, log_bank]
        first_banks = [dense, [sh.bank[7], dense[0], sh.bank[7]], sh.bank[4:7]]

        s = Shared()
        s.state_in = sem("state_in")
        s.constants = sem("constants")
        s.dense_done = sem("dense_done")
        s.qkvo_copied = sem("qkvo_copied")
        s.row_step = sem("row_step")
        s.row_exp = sem("row_exp")
        s.columns_done = sem("columns_done")
        s.columns_ready = sem("columns_ready")
        s.staged = sem("staged")
        s.v_turned = sem("v_turned")
        s.k_turned = sem("k_turned")
        s.logs_done = sem("logs_done")
        s.scores_done = sem("scores_done")
        s.v_copied = sem("v_copied")
        s.weights_ready = sem("weights_ready")
        s.o_exp = sem("o_exp")
        s.o_step = sem("o_step")
        s.keys_ready = sem("keys_ready")
        s.queries_ready = sem("queries_ready")
        s.probs_ready = sem("probs_ready")
        s.nums_done = sem("nums_done")
        s.nums_read = sem("nums_read")
        s.den_step = sem("den_step")
        s.state_added = sem("state_added")
        s.h_squared = sem("h_squared")
        s.mean_ready = sem("mean_ready")
        s.h_log = sem("h_log")
        s.h_exp = sem("h_exp")
        s.h_step = sem("h_step")
        s.h_normed = sem("h_normed")
        s.h_turned = sem("h_turned")
        s.mixed = sem("mixed")
        s.cg_copied = sem("cg_copied")
        s.u_made = sem("u_made")
        s.padded = sem("padded")
        s.y_step = sem("y_step")
        s.z_made = sem("z_made")
        s.z_squared = sem("z_squared")
        s.group_stats = sem("group_stats")
        s.group_mean = sem("group_mean")
        s.group_log = sem("group_log")
        s.group_root = sem("group_root")
        s.group_step = sem("group_step")
        s.conv_made = sem("conv_made")
        s.last_made = sem("last_made")
        s.history = sem("history")
        s.lines_done = sem("lines_done")
        s.lines_ready = sem("lines_ready")
        s.stored = sem("stored")
        block = sh.block


        def arrived(engine, j, before):
            if j < 2:
                engine.wait_ge(m.loaded[j + 1], before * 16 + 16)
            else:
                engine.wait_ge(m.loaded[0], before * 16 + 48)

        def conv_loop(engine, body):
            body(0, True, False)
            with engine.Fori(1, CT - 1) as c:
                body(c, False, False)
            body(CT - 1, False, True)

        @block.sync
        def _(sp):
            def load(tile, j, column):
                sp.wait_ge(m.w_low, tile - 2)
                m.load(sp, (j + 1) % 3, column)

            load(3, 2, COL_Q + 2 * P)
            sp.wait_ge(sh.norm_low, KT * NORM_FFN2)
            for h in range(HEADS):
                part = slice((h % 2) * DK, (h % 2 + 1) * DK)
                sp.dma_start(state_s[part, h // 2, 0:DV], state_C[h]).then_inc(s.state_in, 16)
                sp.dma_start(state_s[part, h // 2, DV:DV + 1], state_n[h]).then_inc(s.state_in, 16)
            with sp.Fori(1, QKVO_TILES // 3) as i:
                for j in range(3):
                    load(i * 3 + (1 + j), j, i * (3 * P) + (COL_Q + j * P))
            with sp.Fori(1, CT + 1) as n:
                for j, first in enumerate((CONV_W, 2 * CONV_W, 0)):
                    load(n * 3 + (QKVO_TILES - 2 + j), j, n * P + (first - P))
            for d in range(3):
                sp.wait_ge(m.w_low, QKVO_TILES + 3 * CT + d - 1)
                o.load(sp, d)
            sp.wait_ge(s.staged, 3 * GROUPS)
            for b in range(BLOCKS):
                sp.dma_start(sh.x[:, 0:KT, block_columns(b)], x_parked[:, :, block_columns(b)]
                             ).then_inc(o.x_in[b], 16)
            for d in range(3, 6):
                o.load(sp, d)
            sp.wait_ge(s.state_added, GROUPS)
            n = 0
            for which, (_, C, n_, m_) in enumerate(((p_conv, p_C, p_n, p_m), (s_conv, s_C, s_n, s_m))):
                state = (state_p, state_s)[which]
                for h in range(HEADS):
                    part = slice((h % 2) * DK, (h % 2 + 1) * DK)
                    sp.dma_start(C[h], state[part, h // 2, 0:DV]).then_inc(s.stored, 16)
                    sp.dma_start(n_[h], state[part, h // 2, DV:DV + 1]).then_inc(s.stored, 16)
                sp.dma_start(m_, m_out[:, which:which + 1]).then_inc(s.stored, 16)
                n += 2 * HEADS + 1
            sp.wait_ge(s.lines_ready, 1)
            for which, conv in enumerate((p_conv, s_conv)):
                sp.dma_start(conv, conv_lines[2 * CT * which:2 * CT * (which + 1), :]).then_inc(s.stored, 16)
                n += 1
            for d in range(6, KT):
                o.load(sp, d)
            sp.wait_ge(s.stored, 16 * n)

        @block.gpsimd
        def _(pool):
            pool.wait_ge(sh.norm_low, KT * NORM_FFN2)
            for n, part in enumerate((values[:, :, DV:DV + 1], state_p[:, :, :], rows[0:HEADS, ROW_KEEP, :],
                                      rows[0:HEADS, ROW_ENM, :], max_before[:, 1:2], staged_q[:, :, :])):
                pool.memset(part, 1.0 if n in (0, 2) else 0.0).then_inc(s.constants, 1)
            pool.wait_ge(s.constants, 6)
            pool.memset(rows[0:HEADS, ROW_KEEP, 0:TOKENS:CHUNK], 0.0).then_inc(s.constants, 1)

            def stage(g, t0, n):
                if not (isinstance(g, int) and g == 0):
                    pool.wait_ge(s.scores_done, g)
                    pool.wait_ge(s.queries_ready, g)
                if not (isinstance(g, int) and g == 0):
                    pool.wait_ge(s.staged, g * 3)
                for e in range(2):
                    part = slice(e * DK, (e + 1) * DK)
                    pool.tensor_copy(staged_q[part, e:HEADS:2, 0:n], sh.x[part, 0:PAIRS, bass.ds(t0, n)]
                                     ).then_inc(s.staged, 1)
                    pool.wait_ge(s.staged, g * 3 + (e + 1))
                pool.tensor_copy(staged_kv[:, :, 0:n], sh.x[:, PAIRS:KT, bass.ds(t0, n)]).then_inc(s.staged, 1)

            pool.wait_ge(s.qkvo_copied, KT * BLOCKS)
            stage(0, SEQ, DEC_SEQ)
            with pool.Fori(0, CHUNKS) as c:
                stage(c + 1, c * CHUNK, CHUNK)

        @block.scalar
        def _(act):
            def copy(t, b, bank):
                act.activation(sh.x[:, bass.ds(t, 1), block_columns(b)].rearrange("p a n -> p (a n)"),
                               bank[:, 0:BLK], ACT.Copy).then_inc(s.qkvo_copied, 1)

            def first_copy(t, b):
                act.wait_ge(s.dense_done, 3 * b + t + 2)
                copy(t, b, first_banks[t][b])

            act.wait_ge(m.parked[0], 16)
            first_copy(0, 0)
            norm_act(act, sh, NORM_MIX + 2)
            first_copy(1, 0)
            act.wait_ge(m.parked[1], 16)
            first_copy(0, 1)
            first_copy(1, 1)
            act.wait_ge(s.dense_done, 3 * BLOCKS - 2)
            arrived(act, 2, 0)
            m.high(act, 0)
            row = rows[0:HEADS, ROW_M, 0:TOKENS]
            act.wait_ge(s.row_step, 3)
            act.activation(row, row, ACT.Exp, scale=-1.0).then_inc(s.row_exp, 1)
            act.wait_ge(s.row_exp, 1)
            act.activation(row, row, ACT.Ln, bias=1.0).then_inc(s.row_exp, 1)
            act.wait_ge(m.parked[2], 16)
            first_copy(0, 2)
            arrived(act, 0, 1)
            m.high(act, 1)
            first_copy(1, 2)
            arrived(act, 1, 1)
            m.high(act, 2)

            def copies(i, js):
                for j in js:
                    for b in range(BLOCKS):
                        act.wait_ge(s.dense_done, i * 9 + (3 * j + BLOCKS + b + 1))
                        copy(i * 3 + j, b, dense[b])
                    arrived(act, j, i + 1)
                    m.high(act, (j + 1) % 3)

            copies(0, (2,))
            with act.Fori(1, QKVO_TILES // 3 - 1) as i:
                copies(i, range(3))
            act.wait_ge(s.row_step, ROW_STEPS)
            for dst, src, scale in ((row_inter[:, :], row_inter[:, :], 1.0),
                                    (rows[0:HEADS, ROW_WK, 0:TOKENS], rows[0:HEADS, ROW_WK, 0:TOKENS], 1.0),
                                    (rows[0:HEADS, ROW_ENM, 0:TOKENS], rows[0:HEADS, ROW_M, 0:TOKENS], -1.0),
                                    (decay_row[:, :], decay_row[:, :], 1.0)):
                act.activation(dst, src, ACT.Exp, scale=scale).then_inc(s.row_exp, 1)
            act.wait_ge(s.columns_ready, 2)

            def stage_a(g, n):
                first = isinstance(g, int) and g == 0
                act.wait_ge(s.v_turned, g + 1)
                if not first:
                    act.wait_ge(s.nums_done, g)
                act.activation(values[0:n, :, 0:DV], v_bank[0:n, :].rearrange("s (h v) -> s h v", v=DV), ACT.Copy
                               ).then_inc(s.v_copied, 1)
                act.wait_ge(s.logs_done, g + 1)
                for h in range(HEADS):
                    e = act.activation(probs[0:n, h, 0:n], log_bank[0:n, h * CHUNK:h * CHUNK + n], ACT.Exp,
                                       bias=by_token[0:n, bass.ds(g * (KINDS_COL * HEADS) + h, 1)])
                e.then_inc(s.weights_ready, 1)

            def gate(g, t0, n):
                if not (isinstance(g, int) and g == 0):
                    act.wait_ge(s.mixed, g)
                act.activation(o_gate[:, :, 0:n], sh.x[:, KT:12, bass.ds(t0, n)], ACT.Exp, scale=-1.0
                               ).then_inc(s.o_exp, 1)

            def stage_b(g, n):
                first = isinstance(g, int) and g == 0
                act.wait_ge(s.nums_read, g + 1)
                for h in range(HEADS):
                    if h or not first:
                        act.wait_ge(s.h_squared, g * HEADS + h)
                    act.activation(h_sq[0:n, :], h_tok[0:n, h, :], ACT.Square, accum_out=sq_sum[0:n, h:h + 1]
                                   ).then_inc(s.h_squared, 1)
                act.wait_ge(s.mean_ready, g + 1)
                act.activation(h_work[0:n, :], sq_sum[0:n, :], ACT.Ln).then_inc(s.h_log, 1)
                act.wait_ge(s.h_log, g + 1)
                act.activation(h_root[0:n, :], h_work[0:n, :], ACT.Exp, scale=-0.5).then_inc(s.h_exp, 1)

            def roots(c):
                act.wait_ge(s.group_mean, c * 3 + 3)
                act.activation(root_work, mean_square, ACT.Ln).then_inc(s.group_log, 1)
                act.wait_ge(s.group_log, c + 1)
                act.activation(inv_rms, root_work, ACT.Exp, scale=-0.5).then_inc(s.group_root, 1)

            def conv_tile(c, first, last):
                even, odd = c * 2 + 1, c * 2 + 2

                def cg(b):
                    act.wait_ge(s.dense_done, c * 9 + (FIRST_CONV + b + 1))
                    if not first:
                        act.wait_ge(s.u_made, c * 3)
                    act.activation(rows[:, CONV_C, block_columns(b)], dense[b][:, 0:BLK], ACT.Copy
                                   ).then_inc(s.cg_copied, 1)

                def z_square(b):
                    act.wait_ge(s.z_made, c * 3 + (b + 1))
                    if not first:
                        act.wait_ge(s.conv_made, c)
                    act.activation(rows[:, CONV_SQ, block_columns(b)], rows[:, CONV_Z, block_columns(b)], ACT.Square
                                   ).then_inc(s.z_squared, 1)

                def next_high(j):
                    if not last:
                        act.wait_ge(s.dense_done, c * 9 + (FIRST_CONV + 3 * (j + 1)))
                        arrived(act, j, c + 5)
                        m.high(act, (j + 1) % 3)

                if not first:
                    roots(c - 1)
                cg(0)
                stage_a(even, CHUNK)
                cg(1)
                if first:
                    gate(0, SEQ, DEC_SEQ)
                cg(2)
                gate(even, c * (2 * CHUNK), CHUNK)
                next_high(0)
                stage_b(even, CHUNK)
                stage_a(odd, CHUNK)
                next_high(1)
                gate(odd, c * (2 * CHUNK) + CHUNK, CHUNK)
                z_square(0)
                stage_b(odd, CHUNK)
                z_square(1)
                z_square(2)
                next_high(2)

            stage_a(0, DEC_SEQ)
            copies(QKVO_TILES // 3 - 1, (0,))
            stage_b(0, DEC_SEQ)
            copies(QKVO_TILES // 3 - 1, (1, 2))
            act.wait_ge(s.qkvo_copied, QKVO_TILES * BLOCKS)
            conv_loop(act, conv_tile)
            act.wait_ge(s.dense_done, BLOCKS * (1 + QKVO_TILES + 3 * CT))
            o.w_high(act, 0)
            o.w_high(act, 1)
            o.mix_high_of(act, 0, (0, 1, 2))
            roots(CT - 1)
            act.wait_ge(s.mixed, GROUPS)
            o.mix_high_of(act, 0, (3, 4, 5, 6))
            for b in range(BLOCKS):
                if b:
                    o.mix_high_of(act, b, range(7))
                act.wait_ge(s.last_made, b + 1)
                o.mix_high_of(act, b, (7,))
                if b < 2:
                    for d in ((2,), (3, 4, 5))[b]:
                        o.w_high(act, d)

        @block.vector
        def _(dve):
            def low(j, tile):
                m.low(dve, (j + 1) % 3, tile)

            norm_dve(dve, sh, NORM_MIX + 2, num_bank, V_MIX)

            a, wk, m_, enm, keep = (rows[0:HEADS, r, 0:TOKENS] for r in (ROW_A, ROW_WK, ROW_M, ROW_ENM, ROW_KEEP))
            step = 0

            def row(instruction):
                nonlocal step
                step += 1
                instruction.then_inc(s.row_step, 1)
                dve.wait_ge(s.row_step, step)

            dve.wait_ge(m.bias_in, 48)
            dve.wait_ge(s.dense_done, 3 * BLOCKS - 2)
            for which, dst in ((0, a), (1, wk)):
                part = slice(32 * which, 32 * which + HEADS)
                for b in range(BLOCKS):
                    last = dve.tensor_scalar(dst[:, block_columns(b)], first_banks[2][b][part, 0:BLK],
                                             gate_bias[part, :], None, ALU.add)
                row(last)
            row(dve.scalar_tensor_tensor(m_, wk, -1.0, wk, ALU.mult, ALU.max))
            low(2, 3)
            dve.wait_ge(s.row_exp, 2)
            row(dve.scalar_tensor_tensor(wk, wk, 0.0, m_, ALU.min, ALU.subtract))
            dve.wait_ge(s.constants, 7)
            row(dve.tensor_tensor_scan(m_, keep, wk, 0.0, ALU.mult, ALU.add))
            row(dve.tensor_tensor(a, a, m_, ALU.subtract))
            row(dve.tensor_copy(enm[:, CHUNK:SEQ:CHUNK], m_[:, CHUNK - 1:SEQ - 1:CHUNK]))
            row(dve.tensor_tensor_scan(row_max[:, 0:SEQ], enm[:, 0:SEQ], a[:, 0:SEQ], 0.0, ALU.add, ALU.max))
            row(dve.tensor_tensor_scan(row_max[:, SEQ:TOKENS], enm[:, SEQ:TOKENS], a[:, SEQ:TOKENS],
                                       max_before[:, 0:1], ALU.add, ALU.max))
            row(dve.tensor_tensor(m_, m_, row_max[:, :], ALU.add))
            low(0, 4)
            row(dve.tensor_copy(m_out[:, 0:1], m_[:, SEQ - 1:SEQ]))
            row(dve.tensor_copy(m_out[:, 1:2], m_[:, TOKENS - 1:TOKENS]))
            row(dve.tensor_copy(max_before[:, 2:GROUPS], m_[:, CHUNK - 1:SEQ - 1:CHUNK]))
            row(dve.tensor_copy(max_last[:, 1:GROUPS], row_max[:, CHUNK - 1:SEQ:CHUNK]))
            row(dve.tensor_copy(max_last[:, 0:1], row_max[:, TOKENS - 1:TOKENS]))
            low(1, 5)
            for g0, g1, t0, t1, n in ((1, GROUPS, 0, SEQ, CHUNK), (0, 1, SEQ, TOKENS, DEC_SEQ)):
                spread = [HEADS, g1 - g0, n]
                parts = (x[:, t0:t1].rearrange("h (g t) -> h g t", t=n) for x in (row_inter, row_max, wk, a))
                inter_v, max_v, wk_v, a_v = parts
                row(dve.tensor_tensor(inter_v, max_before[:, g0:g1].unsqueeze(2).to_broadcast(spread), max_v,
                                      ALU.subtract))
                row(dve.tensor_tensor(wk_v, a_v, max_last[:, g0:g1].unsqueeze(2).to_broadcast(spread),
                                      ALU.subtract))
            row(dve.tensor_tensor(decay_row[:, :], max_before[:, :], max_last[:, :], ALU.subtract))
            assert step == ROW_STEPS

            low(2, 6)
            with dve.Fori(1, QKVO_TILES // 3 - 1) as i:
                for j in range(3):
                    low(j, i * 3 + (4 + j))
            dve.wait_ge(s.columns_done, 1)
            sample, end = KINDS_COL * HEADS, GROUPS * KINDS_COL * HEADS
            dve.tensor_copy(by_token[0:DEC_SEQ, 0:sample], num_bank[0:DEC_SEQ, 0:sample])
            dve.tensor_copy(by_token[:, sample:end], num_bank[:, sample:end]).then_inc(s.columns_ready, 1)
            dve.tensor_scalar(decay[:, :], score_bank[:, 0:PAIRS * GROUPS], float(DK) ** 0.5, None, ALU.mult
                              ).then_inc(s.columns_ready, 1)
            dve.wait_ge(s.columns_ready, 2)

            def stage_a(g, n):
                first = isinstance(g, int) and g == 0
                dve.wait_ge(s.k_turned, g + 1)
                if not first:
                    dve.wait_ge(s.nums_done, g)
                column = g * (KINDS_COL * HEADS)
                dve.tensor_tensor(keys[0:n, :, :], k_bank[0:n, 0:HEADS * DK].rearrange("s (h d) -> s h d", d=DK),
                                  by_token[0:n, bass.ds(column + HEADS, HEADS)].unsqueeze(2).to_broadcast([n, HEADS, DK]),
                                  ALU.mult).then_inc(s.keys_ready, 1)
                inter = k_bank[:, 2 * P:4 * P].rearrange("d (p t) -> d p t", t=P)[:, :, 0:n]
                dve.tensor_tensor(queries[:, :, 0:n].rearrange("d (p e) t -> d p e t", e=2),
                                  staged_q[:, :, 0:n].rearrange("d (p e) t -> d p e t", e=2),
                                  inter.unsqueeze(2).to_broadcast([P, PAIRS, 2, n]),
                                  ALU.mult).then_inc(s.queries_ready, 1)
                dve.wait_ge(s.weights_ready, g + 1)
                dve.wait_ge(s.scores_done, g + 1)
                dve.scalar_tensor_tensor(probs[0:n, :, 0:n],
                                         score_bank[0:n, :].rearrange("s (h t) -> s h t", t=CHUNK)[:, :, 0:n],
                                         float(DK) ** -0.5, probs[0:n, :, 0:n], ALU.mult, ALU.mult
                                         ).then_inc(s.probs_ready, 1)

            def gate(g, n):
                dve.wait_ge(s.o_exp, g + 1)
                dve.tensor_scalar(o_gate[:, :, 0:n], o_gate[:, :, 0:n], 1.0, None, ALU.add).then_inc(s.o_step, 1)
                dve.wait_ge(s.o_step, g * 2 + 1)
                dve.reciprocal(o_gate[:, :, 0:n], o_gate[:, :, 0:n]).then_inc(s.o_step, 1)

            def stage_b(g, n, state):
                first = isinstance(g, int) and g == 0
                dve.wait_ge(s.nums_done, g + 1)
                column = g * (KINDS_COL * HEADS) + 2 * HEADS
                views = [bank[0:n, 0:2 * (DV + 1)].rearrange("t (h v) -> t h v", v=DV + 1) for bank in numerators]
                if not first:
                    dve.wait_ge(s.h_normed, g)
                    dve.wait_ge(s.h_turned, g)
                for p, view in enumerate(views):
                    last = dve.scalar_tensor_tensor(
                        den[0:n, 2 * p:2 * p + 2], view[:, :, DV:DV + 1].rearrange("t h a -> t (h a)"), -1.0,
                        by_token[0:n, bass.ds(column + 2 * p, 2)], ALU.mult, ALU.max)
                last.then_inc(s.den_step, 1)
                dve.wait_ge(s.den_step, g * 3 + 1)
                for p, view in enumerate(views):
                    last = dve.tensor_tensor(
                        den[0:n, 2 * p:2 * p + 2], view[:, :, DV:DV + 1].rearrange("t h a -> t (h a)"),
                        den[0:n, 2 * p:2 * p + 2], ALU.max)
                last.then_inc(s.den_step, 1)
                dve.wait_ge(s.den_step, g * 3 + 2)
                dve.reciprocal(den[0:n, :], den[0:n, :]).then_inc(s.den_step, 1)
                dve.wait_ge(s.den_step, g * 3 + 3)
                for p, view in enumerate(views):
                    last = dve.tensor_tensor(h_tok[0:n, 2 * p:2 * p + 2, :], view[:, :, 0:DV],
                                             den[0:n, 2 * p:2 * p + 2].unsqueeze(2).to_broadcast([n, 2, DV]),
                                             ALU.mult)
                last.then_inc(s.nums_read, 1)
                for p, bank in enumerate((v_bank, k_bank)):
                    for e in range(2):
                        part = slice(e * DK, (e + 1) * DK)
                        last = dve.scalar_tensor_tensor(
                            state[part, p, :], state[part, p, :], decay[part, bass.ds(g + p * GROUPS, 1)],
                            bank[part, e * (DV + 1):(e + 1) * (DV + 1)], ALU.mult, ALU.add)
                last.then_inc(s.state_added, 1)

            def stage_norm(g, n):
                dve.wait_ge(s.h_squared, (g + 1) * HEADS)
                dve.tensor_scalar(sq_sum[0:n, :], sq_sum[0:n, :], 1.0 / DV, EPS, ALU.mult, ALU.add
                                  ).then_inc(s.mean_ready, 1)
                dve.wait_ge(s.h_exp, g + 1)
                dve.tensor_tensor(h_work[0:n, :], h_root[0:n, :], h_root[0:n, :], ALU.mult).then_inc(s.h_step, 1)
                dve.wait_ge(s.h_step, g * 3 + 1)
                dve.scalar_tensor_tensor(h_work[0:n, :], h_work[0:n, :], -0.5, sq_sum[0:n, :], ALU.mult, ALU.mult
                                         ).then_inc(s.h_step, 1)
                dve.wait_ge(s.h_step, g * 3 + 2)
                dve.scalar_tensor_tensor(h_root[0:n, :], h_work[0:n, :], 1.5, h_root[0:n, :], ALU.add, ALU.mult
                                         ).then_inc(s.h_step, 1)
                dve.wait_ge(s.h_step, g * 3 + 3)
                dve.tensor_tensor(h_tok[0:n, :, :], h_tok[0:n, :, :],
                                  h_root[0:n, :].unsqueeze(2).to_broadcast([n, HEADS, DV]), ALU.mult
                                  ).then_inc(s.h_normed, 1)

            def stage_c(g, t0, n):
                dve.wait_ge(s.h_turned, g + 1)
                dve.wait_ge(s.o_step, g * 2 + 2)
                for h in range(HEADS):
                    last = dve.scalar_tensor_tensor(
                        sh.x[:, KT + h, bass.ds(t0, n)], turn_bank[:, h * CHUNK:h * CHUNK + n],
                        sh.vectors[:, V_GMLSTM + h:V_GMLSTM + h + 1], o_gate[:, h, 0:n], ALU.mult, ALU.mult)
                last.then_inc(s.mixed, 1)

            def group_norm(c, cols, step, made):
                dve.wait_ge(s.group_root, c + 1)
                dve.tensor_tensor(root_work[:, cols], inv_rms[:, cols], inv_rms[:, cols], ALU.mult
                                  ).then_inc(s.group_step, 1)
                dve.wait_ge(s.group_step, step + 1)
                dve.scalar_tensor_tensor(root_work[:, cols], root_work[:, cols], -0.5, mean_square[:, cols],
                                         ALU.mult, ALU.mult).then_inc(s.group_step, 1)
                dve.wait_ge(s.group_step, step + 2)
                dve.scalar_tensor_tensor(inv_rms[:, cols], root_work[:, cols], 1.5, inv_rms[:, cols],
                                         ALU.add, ALU.mult).then_inc(s.group_step, 1)
                dve.wait_ge(s.group_step, step + 3)
                dve.scalar_tensor_tensor(conv_out[:, bass.ds(c, 1), cols].rearrange("p a n -> p (a n)"),
                                         rows[:, CONV_Z, cols], sh.vectors[:, bass.ds(c + V_GCONV, 1)],
                                         inv_rms[:, cols], ALU.mult, ALU.mult).then_inc(made, 1)

            def conv_tile(c, first, last_tile):
                even, odd = c * 2 + 1, c * 2 + 2
                u, y, z = rows[:, CONV_U, :], rows[:, CONV_Y, :], rows[:, CONV_Z, :]

                def pad():
                    dve.memset(u[:, 0:2], 0.0)
                    dve.tensor_copy(u[:, SEQ + 2:SEQ + 4].unsqueeze(2),
                                    sh.vectors[:, V_CACHE:V_END].rearrange("p (r c) -> p r c", c=CT)[:, :, bass.ds(c, 1)]
                                    ).then_inc(s.padded, 1)

                def u_of(b):
                    dve.wait_ge(s.dense_done, c * 9 + (FIRST_CONV + 3 + b + 1))
                    dve.wait_ge(s.cg_copied, c * 3 + (b + 1))
                    for cols, padded, of_block in u_parts(b):
                        last = dve.tensor_tensor(u[:, padded], rows[:, CONV_C, cols], dense[b][:, of_block], ALU.mult)
                    last.then_inc(s.u_made, 1)

                def conv():
                    dve.wait_ge(s.u_made, c * 3 + 3)
                    dve.wait_ge(s.padded, c + 1)
                    if not first:
                        dve.wait_ge(s.z_made, c * 3)
                    w = [sh.vectors[:, bass.ds(c + (V_CONVW + k * CT), 1)] for k in range(3)]
                    dve.tensor_scalar(y[:, 2:PADDED], u[:, 2:PADDED], w[2], sh.vectors[:, bass.ds(c + V_CONVB, 1)],
                                      ALU.mult, ALU.add).then_inc(s.y_step, 1)
                    for k in (1, 0):
                        dve.wait_ge(s.y_step, c * 3 + (2 - k))
                        dve.scalar_tensor_tensor(y[:, 2:PADDED], u[:, k:PADDED - 2 + k], w[k], y[:, 2:PADDED],
                                                 ALU.mult, ALU.add).then_inc(s.y_step, 1)
                    out = conv_last[:, :, bass.ds(c, 1)]
                    dve.tensor_copy(out[:, 0:2, :], u[:, SEQ:SEQ + 2].unsqueeze(2))
                    dve.tensor_copy(out[:, 2:4, :], u[:, PADDED - 2:PADDED].unsqueeze(2)).then_inc(s.history, 1)

                def z_of(b):
                    dve.wait_ge(s.dense_done, c * 9 + (FIRST_CONV + 6 + b + 1))
                    dve.wait_ge(s.y_step, c * 3 + 3)
                    if not first:
                        dve.wait_ge(s.z_squared, c * 3)
                    for cols, padded, of_block in u_parts(b):
                        last = dve.tensor_tensor(z[:, cols], y[:, padded], dense[b][:, of_block], ALU.mult)
                    last.then_inc(s.z_made, 1)

                def group_mean(b):
                    dve.wait_ge(s.group_stats, c * 3 + (b + 1))
                    if b == 0:
                        dve.wait_ge(s.z_made, c * 3 + 3)
                    dve.tensor_scalar(mean_square[:, block_columns(b)], dense[b][:, 0:BLK], EPS, None, ALU.add
                                      ).then_inc(s.group_mean, 1)

                def next_low(j):
                    if not last_tile:
                        low(j, c * 3 + (QKVO_TILES + 4 + j))

                stage_a(even, CHUNK)
                if first:
                    gate(0, DEC_SEQ)
                    stage_c(0, SEQ, DEC_SEQ)
                else:
                    stage_c(c * 2, c * (2 * CHUNK) - CHUNK, CHUNK)
                    group_norm(c - 1, slice(0, TOKENS), c * 3 - 3, s.conv_made)
                    dve.wait_ge(s.conv_made, c)
                pad()
                next_low(0)
                stage_b(even, CHUNK, state_p)
                gate(even, CHUNK)
                stage_norm(even, CHUNK)
                u_of(0)
                stage_a(odd, CHUNK)
                u_of(1)
                u_of(2)
                stage_c(even, c * (2 * CHUNK), CHUNK)
                next_low(1)
                conv()
                z_of(0)
                stage_b(odd, CHUNK, state_p)
                gate(odd, CHUNK)
                stage_norm(odd, CHUNK)
                z_of(1)
                z_of(2)
                for b in range(BLOCKS):
                    group_mean(b)
                next_low(2)

            dve.wait_ge(s.state_in, 16 * 2 * HEADS)
            stage_a(0, DEC_SEQ)
            last = QKVO_TILES - 3
            low(0, last + 4)
            stage_b(0, DEC_SEQ, state_s)
            stage_norm(0, DEC_SEQ)
            low(1, last + 5)
            low(2, last + 6)
            conv_loop(dve, conv_tile)
            o.w_low(dve, 0)
            o.w_low(dve, 1)
            o.mix_low_of(dve, 0, (0, 1, 2))
            stage_c(GROUPS - 1, SEQ - CHUNK, CHUNK)
            o.mix_low_of(dve, 0, (3, 4, 5, 6))
            for b in range(BLOCKS):
                group_norm(CT - 1, block_columns(b), 3 * (CT - 1) + 3 * b, s.last_made)
                o.mix_low_of(dve, b, (range(7) if b else ()))
                o.mix_low_of(dve, b, (7,))
                if b < 2:
                    for d in ((2,), (3, 4, 5))[b]:
                        o.w_low(dve, d)
                if b == 1:
                    dve.wait_ge(o.x_in[0], 16)
                    o.add(dve, 0, 0)
                    o.add(dve, 0, 1)
            dve.wait_ge(s.lines_done, 1)
            dve.tensor_copy(conv_lines[:, :], num_bank[0:4 * CT, 0:P]).then_inc(s.lines_ready, 1)

        @block.tensor
        def _(pe):
            def product(b, j, bank=None):
                for k in range(KT):
                    col = slice(k * P, (k + 1) * P)
                    last = products(pe, (dense[b] if bank is None else bank)[:, 0:BLK], sh.w_hi[(j + 1) % 3][:, col],
                                    sh.w_lo[(j + 1) % 3][:, col], sh.in_hi[:, k, block_columns(b)],
                                    sh.in_lo[:, k, block_columns(b)], k == 0, k == KT - 1)
                last.then_inc(s.dense_done, 1)

            pe.wait_ge(sh.x_added, FT // 2 * BLOCKS * KT)
            for b in range(BLOCKS):
                pe.wait_ge(sh.norm_low, KT * (NORM_MIX + b + 1))
                pe.wait_ge(m.w_low, 1)
                product(b, 2, first_banks[2][b])
                pe.wait_ge(m.w_low, 2)
                product(b, 0, first_banks[0][b])
                if b == 0:
                    norm_stats(pe, sh, NORM_MIX + 2, num_bank)
                pe.wait_ge(m.w_low, 3)
                if b == 1:
                    pe.wait_ge(s.qkvo_copied, 1)
                if b == 2:
                    pe.wait_ge(s.qkvo_copied, 2)
                product(b, 1, first_banks[1][b])

            def qkvo_tile(n, j):
                pe.wait_ge(m.w_low, n + 2)
                for b in range(BLOCKS):
                    pe.wait_ge(s.qkvo_copied, n * 3 + (b - 2))
                    product(b, j)

            qkvo_tile(2, 2)
            with pe.Fori(1, QKVO_TILES // 3 - 1) as i:
                for j in range(3):
                    qkvo_tile(i * 3 + j, j)

            pe.wait_ge(s.row_exp, 6)
            pe.wait_ge(s.row_step, ROW_STEPS)
            for g in range(GROUPS):
                t0, n = (SEQ, DEC_SEQ) if g == 0 else ((g - 1) * CHUNK, CHUNK)
                for kind, r in enumerate((ROW_A, ROW_WK, ROW_ENM)):
                    at = (g * KINDS_COL + kind) * HEADS
                    pe.transpose(num_bank[0:n, at:at + HEADS], rows[0:HEADS, r, t0:t0 + n],
                                 sh.ident[0:HEADS, 0:HEADS])
            for p in range(PAIRS):
                last = pe.matmul(score_bank[:, p * GROUPS:(p + 1) * GROUPS], sh.pair_rows[:, p, :], decay_row[:, :],
                                 start=True, stop=True)
            last.then_inc(s.columns_done, 1)
            pe.wait_ge(s.columns_ready, 2)
            pe.wait_ge(s.constants, 7)

            def stage_a(g, t0, n):
                pe.wait_ge(s.staged, g * 3 + 3)
                if not (isinstance(g, int) and g == 0):
                    pe.wait_ge(s.state_added, g)
                for h in range(HEADS):
                    last = pe.transpose(v_bank[0:n, h * DV:(h + 1) * DV], staged_kv[:, PAIRS + h, 0:n], sh.ident[:, :])
                last.then_inc(s.v_turned, 1)
                for p in range(PAIRS):
                    pe.transpose(k_bank[0:n, p * P:(p + 1) * P], staged_kv[:, p, 0:n], sh.ident[:, :])
                for p in range(PAIRS):
                    at = (2 + p) * P
                    last = pe.matmul(k_bank[:, at:at + n], sh.pair_rows[:, p, :], row_inter[:, bass.ds(t0, n)],
                                     start=True, stop=True)
                last.then_inc(s.k_turned, 1)
                if not (isinstance(g, int) and g == 0):
                    pe.wait_ge(s.nums_read, g)
                for h in range(HEADS):
                    out = log_bank[0:n, h * CHUNK:h * CHUNK + n]
                    pe.matmul(out, sh.head_row[:, h, 0:n], row_max[:, bass.ds(t0, n)], start=True, stop=False)
                    last = pe.matmul(out, sh.ident16[0:n, 0:n], sh.mask[0:n, 0:n], start=False, stop=True)
                last.then_inc(s.logs_done, 1)
                if not (isinstance(g, int) and g == 0):
                    pe.wait_ge(s.probs_ready, g)
                for h in range(HEADS):
                    last = pe.matmul(score_bank[0:n, h * CHUNK:h * CHUNK + n], staged_kv[:, h // 2, 0:n],
                                     staged_q[:, h, 0:n], start=True, stop=True)
                last.then_inc(s.scores_done, 1)

            def stage_b(g, n, state):
                pe.wait_ge(s.v_copied, g + 1)
                pe.wait_ge(s.keys_ready, g + 1)
                pe.wait_ge(s.queries_ready, g + 1)
                pe.wait_ge(s.probs_ready, g + 1)
                if not (isinstance(g, int) and g == 0):
                    pe.wait_ge(s.mixed, g)
                for h in range(HEADS):
                    out = numerators[h // 2][0:n, (h % 2) * (DV + 1):(h % 2 + 1) * (DV + 1)]
                    pe.matmul(out, probs[0:n, h, 0:n], values[0:n, h, :], start=True, stop=False)
                    pe.matmul(out, queries[:, h, 0:n], state[:, h // 2, :], start=False, stop=True)
                for p, bank in enumerate((v_bank, k_bank)):
                    last = pe.matmul(bank[:, 0:2 * (DV + 1)], keys[0:n, 2 * p:2 * p + 2, :],
                                     values[0:n, 2 * p:2 * p + 2, :], start=True, stop=True)
                last.then_inc(s.nums_done, 1)

            def stage_c(g, n):
                pe.wait_ge(s.h_normed, g + 1)
                for h in range(HEADS):
                    last = pe.transpose(turn_bank[:, h * CHUNK:h * CHUNK + n], h_tok[0:n, h, :], sh.ident[0:n, 0:n])
                last.then_inc(s.h_turned, 1)

            def conv_tile(c, first, _):
                even, odd = c * 2 + 1, c * 2 + 2

                def cg(b):
                    if first:
                        pe.wait_ge(s.qkvo_copied, (QKVO_TILES - 1) * BLOCKS + b + 1)
                    else:
                        pe.wait_ge(s.group_mean, c * 3 + (b - 2))
                    product(b, 0)

                def xin(b):
                    pe.wait_ge(s.cg_copied, c * 3 + (b + 1))
                    product(b, 1)

                def bg(b):
                    pe.wait_ge(s.u_made, c * 3 + (b + 1))
                    product(b, 2)

                def stats(b):
                    pe.wait_ge(s.z_squared, c * 3 + (b + 1))
                    pe.matmul(dense[b][:, 0:BLK], sh.mean_group[:, :], rows[:, CONV_SQ, block_columns(b)],
                              start=True, stop=True).then_inc(s.group_stats, 1)

                pe.wait_ge(m.w_low, c * 3 + (QKVO_TILES + 2))
                cg(0)
                stage_a(even, c * (2 * CHUNK), CHUNK)
                cg(1)
                if first:
                    stage_c(0, DEC_SEQ)
                else:
                    stage_c(c * 2, CHUNK)
                cg(2)
                stage_b(even, CHUNK, state_p)
                pe.wait_ge(m.w_low, c * 3 + (QKVO_TILES + 3))
                xin(0)
                stage_a(odd, c * (2 * CHUNK) + CHUNK, CHUNK)
                xin(1)
                xin(2)
                stage_c(even, CHUNK)
                pe.wait_ge(m.w_low, c * 3 + (QKVO_TILES + 4))
                bg(0)
                stage_b(odd, CHUNK, state_p)
                bg(1)
                stats(0)
                bg(2)
                stats(1)
                stats(2)

            pe.wait_ge(s.state_in, 16 * 2 * HEADS)
            stage_a(0, SEQ, DEC_SEQ)
            qkvo_tile(QKVO_TILES - 3, 0)
            stage_b(0, DEC_SEQ, state_s)
            qkvo_tile(QKVO_TILES - 2, 1)
            qkvo_tile(QKVO_TILES - 1, 2)
            conv_loop(pe, conv_tile)
            stage_c(GROUPS - 1, CHUNK)
            pe.wait_ge(s.history, CT)
            pe.wait_ge(s.mixed, GROUPS)
            pe.transpose(num_bank[0:4 * CT, 0:P], conv_last[:, :, :].rearrange("p r c -> p (r c)"), sh.ident[:, :]
                         ).then_inc(s.lines_done, 1)

        sh.norm = next_norm


ROW_STEPS = 20


def out_phase(nc, sh, o, f):
    block = sh.block
    before = {("gate", 0): 2, ("up", 0): 0, ("gate", 1): 1, ("up", 1): 3, ("down", 0): 4, ("down", 1): 5}

    @block.sync
    def _(sp):
        sp.wait_ge(o.low, KT)
        for w, j in FIRST_TILES:
            weight_load(sp, sh, f, w, j, j)

    @block.gpsimd
    def _(pool):
        for b in range(BLOCKS):
            norm_add(pool, sh, NORM_FFN2 + b)

    @block.scalar
    def _(act):
        o.w_high(act, 6)
        o.w_high(act, 7)
        norm_squares(act, sh, NORM_FFN2, o.added, 0)
        norm_squares(act, sh, NORM_FFN2 + 1, o.added, KT)
        norm_act(act, sh, NORM_FFN2)
        for w, j in FIRST_TILES:
            act.wait_ge(o.done, 2 * KT + before[w, j] + 1)
            weight_high(act, sh, f, w, j, 0)
        norm_squares(act, sh, NORM_FFN2 + 2, o.added, 2 * KT)
        norm_act(act, sh, NORM_FFN2 + 1)

    @block.vector
    def _(dve):
        dve.wait_ge(o.x_in[0], 16)
        o.add(dve, 0, 2)
        o.w_low(dve, 6)
        o.add(dve, 0, 3)
        o.w_low(dve, 7)
        for d in range(4, KT):
            o.add(dve, 0, d)
        dve.wait_ge(o.x_in[1], 16)
        for d in range(KT):
            o.add(dve, 1, d)
        dve.wait_ge(o.x_in[2], 16)
        norm_dve(dve, sh, NORM_FFN2, sh.bank[3], V_FFN2)
        for d in range(KT):
            o.add(dve, 2, d)
            if d == 4:
                weight_low(dve, sh, f, "gate", 0, 0)
                weight_low(dve, sh, f, "up", 0, 0)
        for w, j in FIRST_TILES[2:]:
            weight_low(dve, sh, f, w, j, 0)
        norm_dve(dve, sh, NORM_FFN2 + 1, sh.bank[3], V_FFN2)

    @block.tensor
    def _(pe):
        for b in range(BLOCKS):
            pe.wait_ge(o.mix_low, KT * (b + 1))
            for d in range(KT):
                i = b * KT + d
                if b == 0:
                    pe.wait_ge(o.low, d + 1)
                if i >= 4:
                    pe.wait_ge(o.added, i - 3)
                hi, lo = o.w_halves(d)
                for k in range(KT):
                    col = slice(k * P, (k + 1) * P)
                    last = products(pe, sh.bank[4 + i % 4][:, 0:BLK], hi[:, col], lo[:, col],
                                    sh.in_hi[:, k, block_columns(b)], sh.in_lo[:, k, block_columns(b)],
                                    k == 0, k == KT - 1)
                last.then_inc(o.done, 1)
                if d == 3 and b:
                    norm_stats(pe, sh, NORM_FFN2 + b - 1, sh.bank[3])


def encoder_kernel(nc, args, outs):
    with ExitStack() as ctx:
        sh = shared_tensors(nc, ctx)
        sh.block = ctx.enter_context(nc.Block())

        def lines(name, pattern, **sizes):
            return args[name].rearrange(pattern, **sizes)

        vector_rows = [
            (lines("ffn1_norm", "(r p) -> r p", p=P), V_FFN1), (lines("mix_norm", "(r p) -> r p", p=P), V_MIX),
            (lines("ffn2_norm", "(r p) -> r p", p=P), V_FFN2), (lines("final_norm", "(r p) -> r p", p=P), V_FINAL),
            (lines("conv_w", "k (r p) -> (k r) p", p=P), V_CONVW), (lines("conv_b", "(r p) -> r p", p=P), V_CONVB),
            (lines("g_conv", "(r g) d -> r (g d)", g=2), V_GCONV), (args["g_mlstm"], V_GMLSTM),
            (lines("cache_conv", "k (r p) -> (k r) p", p=P), V_CACHE)]

        def columns(ap):
            return ap.rearrange("(n a) -> n a", a=1)

        x_parked = nc.dram_tensor("x_parked", (P, KT, TOKENS), FP32, kind="Internal").ap()
        f1, f2 = (ffn_weights(sh, n, args[f"{n}_w_gate"], args[f"{n}_w_up"], args[f"{n}_w_down"])
                  for n in ("ffn1", "ffn2"))
        m = mixer_weights(sh, args["w_in"], columns(args["b_igate"]), columns(args["b_fgate"]),
                          columns(args["state_m"]), x_parked, f1)
        with ExitStack() as ffn_ctx:
            sh.norm = wide_buffers(sh, lambda n, shape, dt: ffn_ctx.enter_context(nc.sbuf_tensor(f"ffn1_{n}", shape, dt)))
            load_phase(nc, sh, args["x_prompt"], args["x_sample"], vector_rows, f1)
            ffn_phase(nc, sh, "ffn1", f1, (NORM_FFN1 + 1, NORM_FFN1 + 2), V_FFN1, NORM_MIX, V_MIX, m)
        with ExitStack() as mix_ctx:
            with nc.sbuf_tensor("conv_out", [P, CT, TOKENS], FP32) as conv_out:
                pass
            with ExitStack() as hidden_ctx:
                hidden2 = hidden_buffers(nc, "ffn2", hidden_ctx)
            w_last = mix_ctx.enter_context(nc.sbuf_tensor("w_last", [P, CT, TOKENS], FP32R))
            o = out_weights(sh, args["w_out"], conv_out, w_last)

            def heads(ap):
                return [ap[h] for h in range(HEADS)]

            def head_columns(ap):
                return [columns(ap[h]) for h in range(HEADS)]

            def conv_rows(ap):
                return ap.rearrange("r (c p) -> (r c) p", p=P)

            def more_buffers():
                return wide_buffers(sh, lambda n, shape, dt: mix_ctx.enter_context(nc.sbuf_tensor(f"ffn2_{n}", shape, dt)))

            mixer_phase(nc, sh, m, o, heads(args["state_C"]), head_columns(args["state_n"]), x_parked, conv_out,
                        conv_rows(outs["prompt_conv"]), heads(outs["prompt_C"]), head_columns(outs["prompt_n"]),
                        columns(outs["prompt_m"]),
                        conv_rows(outs["sample_conv"]), heads(outs["sample_C"]), head_columns(outs["sample_n"]),
                        columns(outs["sample_m"]), more_buffers)
            out_phase(nc, sh, o, f2)
            ffn_phase(nc, sh, "ffn2", f2, (NORM_FFN2 + 2,), V_FFN2, NORM_FINAL, V_FINAL,
                      hidden_tensors=hidden2)
        final_phase(nc, sh, outs["y_prompt"], outs["y_sample"])


INPUTS = ["x_prompt", "x_sample", "cache_conv", "state_C", "state_n", "state_m", "ffn1_norm", "ffn1_w_gate",
          "ffn1_w_up", "ffn1_w_down", "mix_norm", "w_in", "b_igate", "b_fgate", "conv_w", "conv_b", "g_conv",
          "g_mlstm", "w_out", "ffn2_norm", "ffn2_w_gate", "ffn2_w_up", "ffn2_w_down", "final_norm"]
OUTPUTS = [("y_prompt", (1, SEQ, D_MODEL), 1), ("y_sample", (1, DEC_SEQ, D_MODEL), 1),
           ("prompt_conv", (1, 1, 2, CONV_W), 2), ("prompt_C", (1, 1, HEADS, DK, DV), 2),
           ("prompt_n", (1, 1, HEADS, DK), 2), ("prompt_m", (1, 1, HEADS), 2),
           ("sample_conv", (1, 1, 2, CONV_W), 2), ("sample_C", (1, 1, HEADS, DK, DV), 2),
           ("sample_n", (1, 1, HEADS, DK), 2), ("sample_m", (1, 1, HEADS), 2)]


def kernel(**inputs):
    import concourse.bacc as bacc
    from concourse.bass_utils import run_bass_kernel_spmd

    nc = bacc.Bacc("TRN2", target_bir_lowering=False, num_devices=1, dynamic_dma_scratch_size=1024)

    def inner(ap, ones):
        for _ in range(ones):
            ap = ap[0]
        return ap

    arrays, args, outs = {}, {}, {}
    for name in INPUTS:
        a = np.ascontiguousarray(inputs[name])
        arrays[f"in_{name}"] = a
        ap = nc.dram_tensor(f"in_{name}", a.shape, mybir.dt.from_np(a.dtype), kind="ExternalInput").ap()
        ones = {"final_norm": 0, "cache_conv": 2, "state_C": 2, "state_n": 2, "state_m": 2}.get(name, 1)
        args[name] = inner(ap, ones)
    for name, shape, ones in OUTPUTS:
        outs[name] = inner(nc.dram_tensor(f"out_{name}", shape, FP32, kind="ExternalOutput").ap(), ones)
    encoder_kernel(nc, args, outs)
    r = run_bass_kernel_spmd(nc, [arrays], core_ids=[0])
    return tuple(r.results[0][f"out_{name}"] for name, _, _ in OUTPUTS)
```
